# Optimizing a Trainium2 kernel written in Bass

```python
import jax, jax.numpy as jnp
from jax import lax
import numpy as np

D_MODEL = 1024
BATCH = 1
SEQ = 2048
DEPTH = 2

HEAD_DIM = 64
SB_HEADS = 6
RET_HEADS = 6
MEM_HEADS = 4
MEM_TOKENS = 256
SB_WIDTH = SB_HEADS * HEAD_DIM
RET_WIDTH = RET_HEADS * HEAD_DIM
MEM_WIDTH = MEM_HEADS * HEAD_DIM
MIX_WIDTH = SB_WIDTH + RET_WIDTH + MEM_WIDTH
IN_WIDTH = 4 * SB_WIDTH + 4 * RET_WIDTH + 2 * MEM_WIDTH
Q_BLOCK = 128
RET_CHUNK = 128
ROPE_BASE = 10000.0
EPS = 1e-6

kernel_name = "hybrid_stickbreaking_retention_memory"

def rms_norm(x, g):
    xf = x.astype(jnp.float32)
    y = xf * lax.rsqrt(jnp.mean(xf * xf, axis=-1, keepdims=True) + EPS)
    return (y * g.astype(jnp.float32)).astype(x.dtype)

def split_heads(t, n_heads):
    b, s, _ = t.shape
    return t.reshape(b, s, n_heads, HEAD_DIM).transpose(0, 2, 1, 3)

def merge_heads(t):
    b, h, s, d = t.shape
    return t.transpose(0, 2, 1, 3).reshape(b, s, h * d)

def rotary(t, positions):
    half = t.shape[-1] // 2
    inv_freq = ROPE_BASE ** (-jnp.arange(half, dtype=jnp.float32) / half)
    ang = positions.astype(jnp.float32)[:, None, :, None] * inv_freq
    cos, sin = jnp.cos(ang), jnp.sin(ang)
    tf = t.astype(jnp.float32)
    t1, t2 = tf[..., :half], tf[..., half:]
    return jnp.concatenate([t1 * cos - t2 * sin, t1 * sin + t2 * cos], axis=-1).astype(t.dtype)

def stick_breaking_attention(q, k, v):
    b, h, s, d = q.shape
    nb = s // Q_BLOCK
    qb = q.reshape(b, h, nb, Q_BLOCK, d).transpose(2, 0, 1, 3, 4)
    kf = k.astype(jnp.float32)
    vf = v.astype(jnp.float32)
    scale = d ** -0.5
    key_pos = jnp.arange(s)

    def block(args):
        qblk, b_idx = args
        z = jnp.einsum('bhqd,bhkd->bhqk', qblk.astype(jnp.float32), kf) * scale
        q_pos = b_idx * Q_BLOCK + jnp.arange(Q_BLOCK)
        causal = key_pos[None, :] < q_pos[:, None]
        log_beta = jax.nn.log_sigmoid(z)
        log_keep = jnp.where(causal, jax.nn.log_sigmoid(-z), 0.0)
        later = lax.cumsum(log_keep, axis=3, reverse=True) - log_keep
        w = jnp.where(causal, jnp.exp(log_beta + later), 0.0)
        return jnp.einsum('bhqk,bhkd->bhqd', w, vf)

    out = lax.map(block, (qb, jnp.arange(nb)))
    return out.transpose(1, 2, 0, 3, 4).reshape(b, h, s, d).astype(q.dtype)

def retention_chunkwise(q, k, v):
    b, h, s, d = q.shape
    c = RET_CHUNK
    nc = s // c
    log_gamma = jnp.log(1.0 - 2.0 ** (-5.0 - jnp.arange(h, dtype=jnp.float32)))
    kf = k.astype(jnp.float32) * d ** -0.5

    def chunks(t):
        return t.astype(jnp.float32).reshape(b, h, nc, c, d).transpose(2, 0, 1, 3, 4)

    qc, kc, vc = chunks(q), chunks(kf), chunks(v)
    idx = jnp.arange(c, dtype=jnp.float32)
    diff = idx[:, None] - idx[None, :]
    lg = log_gamma[:, None, None]
    decay_intra = jnp.where(diff >= 0, jnp.exp(lg * jnp.maximum(diff, 0.0)), 0.0)
    q_decay = jnp.exp(log_gamma[:, None] * (idx + 1.0))
    k_decay = jnp.exp(log_gamma[:, None] * (c - 1.0 - idx))
    chunk_decay = jnp.exp(log_gamma * c)

    def step(state, inp):
        qi, ki, vi = inp
        scores = jnp.einsum('bhid,bhjd->bhij', qi, ki) * decay_intra
        intra = jnp.einsum('bhij,bhjd->bhid', scores, vi)
        cross = jnp.einsum('bhid,bhde->bhie', qi, state) * q_decay[None, :, :, None]
        new_state = state * chunk_decay[None, :, None, None] + jnp.einsum(
            'bhjd,bhje->bhde', ki * k_decay[None, :, :, None], vi)
        return new_state, intra + cross

    state0 = jnp.zeros((b, h, d, d), jnp.float32)
    _, out = lax.scan(step, state0, (qc, kc, vc))
    return out.transpose(1, 2, 0, 3, 4).reshape(b, h, s, d)

def memory_cross_attention(q, mk, mv, g_q, g_k):
    qn = rms_norm(q, g_q).astype(jnp.float32)
    kn = rms_norm(mk, g_k).astype(jnp.float32)
    scores = jnp.einsum('bhsd,bhmd->bhsm', qn, kn) * (q.shape[-1] ** -0.5)
    p = jax.nn.softmax(scores, axis=-1)
    return jnp.einsum('bhsm,bhmd->bhsd', p, mv.astype(jnp.float32)).astype(q.dtype)

def setup_inputs(seed: int = 0) -> dict:
    key = jax.random.key(seed)
    ks = jax.random.split(key, 12)
    f32 = jnp.float32
    x = jax.random.normal(ks[0], (BATCH, SEQ, D_MODEL), f32)
    mem = jax.random.normal(ks[1], (BATCH, MEM_TOKENS, D_MODEL), f32)
    offsets = jax.random.randint(ks[2], (BATCH, 1), 0, 1024, dtype=jnp.int32)
    positions = (jnp.arange(SEQ, dtype=jnp.int32)[None, :] + offsets).astype(jnp.int32)
    norm_g = 1.0 + 0.02 * jax.random.normal(ks[3], (DEPTH, D_MODEL), f32)
    w_in = jax.random.normal(ks[4], (DEPTH, D_MODEL, IN_WIDTH), f32) * D_MODEL ** -0.5
    w_out = jax.random.normal(ks[5], (DEPTH, MIX_WIDTH, D_MODEL), f32) * MIX_WIDTH ** -0.5
    mem_norm_g = 1.0 + 0.02 * jax.random.normal(ks[6], (DEPTH, D_MODEL), f32)
    w_mem_kv = jax.random.normal(ks[7], (DEPTH, D_MODEL, 2 * MEM_WIDTH), f32) * D_MODEL ** -0.5
    mem_q_norm_g = 1.0 + 0.02 * jax.random.normal(ks[8], (DEPTH, HEAD_DIM), f32)
    mem_k_norm_g = 1.0 + 0.02 * jax.random.normal(ks[9], (DEPTH, HEAD_DIM), f32)
    ret_norm_g = 1.0 + 0.02 * jax.random.normal(ks[10], (DEPTH, RET_WIDTH), f32)
    return {"x": x, "mem": mem, "positions": positions, "norm_g": norm_g, "w_in": w_in,
            "w_out": w_out, "mem_norm_g": mem_norm_g, "w_mem_kv": w_mem_kv,
            "mem_q_norm_g": mem_q_norm_g, "mem_k_norm_g": mem_k_norm_g, "ret_norm_g": ret_norm_g}

def reference(x, mem, positions, norm_g, w_in, w_out, mem_norm_g, w_mem_kv,
              mem_q_norm_g, mem_k_norm_g, ret_norm_g):
    widths = [SB_WIDTH] * 4 + [RET_WIDTH] * 4 + [MEM_WIDTH] * 2
    split_at = [int(v) for v in np.cumsum(widths)[:-1]]
    b, s, _ = x.shape
    for l in range(DEPTH):
        h = rms_norm(x, norm_g[l])
        proj = jnp.einsum('bsd,de->bse', h, w_in[l])
        (sb_q, sb_k, sb_v, sb_g, ret_q, ret_k, ret_v, ret_g,
         mem_q, mem_g) = jnp.split(proj, split_at, axis=-1)

        sb_o = stick_breaking_attention(split_heads(sb_q, SB_HEADS), split_heads(sb_k, SB_HEADS),
                                        split_heads(sb_v, SB_HEADS))
        sb_o = merge_heads(sb_o) * jax.nn.silu(sb_g)

        rq = rotary(split_heads(ret_q, RET_HEADS), positions)
        rk = rotary(split_heads(ret_k, RET_HEADS), positions)
        ret_o = retention_chunkwise(rq, rk, split_heads(ret_v, RET_HEADS))
        ret_o = ret_o * lax.rsqrt(jnp.mean(ret_o * ret_o, axis=-1, keepdims=True) + EPS)
        ret_o = (merge_heads(ret_o) * ret_norm_g[l].astype(jnp.float32)).astype(x.dtype)
        ret_o = ret_o * jax.nn.silu(ret_g)

        mh = rms_norm(mem, mem_norm_g[l])
        mkv = jnp.einsum('bmd,de->bme', mh, w_mem_kv[l])
        mk, mv = jnp.split(mkv, 2, axis=-1)
        mem_o = memory_cross_attention(split_heads(mem_q, MEM_HEADS), split_heads(mk, MEM_HEADS),
                                       split_heads(mv, MEM_HEADS), mem_q_norm_g[l], mem_k_norm_g[l])
        mem_o = merge_heads(mem_o) * jax.nn.silu(mem_g)

        mixed = jnp.concatenate([sb_o, ret_o, mem_o], axis=-1)
        x = x + jnp.einsum('bse,ed->bsd', mixed, w_out[l])
    return x


_drawn_inputs = setup_inputs


def setup_inputs(seed=0):
    import zlib

    import numpy as np

    out = dict(_drawn_inputs(seed))
    spreads = {}
    factors = {'mem_norm_g': 8.0, 'mem_q_norm_g': 8.0, 'mem_k_norm_g': 8.0, 'ret_norm_g': 5.699}
    for name, (base, spread) in spreads.items():
        noise = np.random.default_rng([zlib.crc32(name.encode()), seed]).standard_normal(out[name].shape)
        drawn = base * np.exp(spread * noise) if base else spread * noise
        out[name] = __import__('jax').numpy.asarray(drawn.astype(out[name].dtype))
    for name, factor in factors.items():
        out[name] = (out[name] * factor).astype(out[name].dtype)
    return out
```

```python
from contextlib import ExitStack

import numpy as np

import concourse.bass as bass
from concourse import mybir

F32 = mybir.dt.float32
F32R = mybir.dt.float32r
I32 = mybir.dt.int32
ALU = mybir.AluOpType
ACT = mybir.ActivationFunctionType
AX = mybir.AxisListType

P = 128
D_MODEL = 1024
SEQ = 2048
DEPTH = 2
HD = 64
SB_HEADS, RET_HEADS, MEM_HEADS = 6, 6, 4
MEM_TOKENS = 256
IN_WIDTH = (4 * SB_HEADS + 4 * RET_HEADS + 2 * MEM_HEADS) * HD
EPS = 1e-6
ROPE_BASE = 10000.0

KC = D_MODEL // P
TILES = SEQ // P
SPAN = 512
SPANS = SEQ // SPAN
NBLK = IN_WIDTH // P
SBP, RETP, MEMP = SB_HEADS // 2, RET_HEADS // 2, MEM_HEADS // 2

_SB, _RET, _MEM = 0, 4 * SBP, 4 * SBP + 4 * RETP
ORDER = list(range(_SB, _SB + 2 * SBP))
RETQ = len(ORDER)
ORDER += range(_RET, _RET + 2 * RETP)
SBV = len(ORDER)
ORDER += range(_SB + 2 * SBP, _SB + 3 * SBP)
RETV = len(ORDER)
ORDER += range(_RET + 2 * RETP, _RET + 3 * RETP)
MEMQ = len(ORDER)
ORDER += range(_MEM, _MEM + MEMP)
GATE0 = len(ORDER)
ORDER += (list(range(_SB + 3 * SBP, _SB + 4 * SBP)) + list(range(_RET + 3 * RETP, _RET + 4 * RETP))
          + list(range(_MEM + MEMP, _MEM + 2 * MEMP)))
KINDS = (("split", 0, RETQ), ("rotate", RETQ, SBV), ("plain", SBV, GATE0), ("gate", GATE0, NBLK))
MIXP = SBP + RETP
ALLP = MIXP + MEMP

C_ID, C_MASK, C_AVG = 0, P, 2 * P
C_DEC = 3 * P
C_QD = C_DEC + RET_HEADS * P
C_KD = C_QD + RETP * P
C_CD = C_KD + RET_HEADS
C_FREQ = C_CD + RETP
C_SIGN = C_FREQ + 1
C_ALL = C_SIGN + 1


def constants():
    c = np.zeros((P, C_ALL), np.float64)
    i = np.arange(P)
    c[:, C_ID:C_ID + P] = np.eye(P)
    c[:, C_MASK:C_MASK + P] = np.where(i[None, :] >= i[:, None], -1e30, 0.0)
    c[:, C_AVG:C_AVG + P] = (i[:, None] // HD == i[None, :] // HD) / HD
    lg = np.log(1.0 - 2.0 ** (-5.0 - np.arange(RET_HEADS)))
    gap = i[None, :] - i[:, None]
    for h in range(RET_HEADS):
        c[:, C_DEC + h * P:C_DEC + (h + 1) * P] = np.where(gap >= 0, np.exp(lg[h] * np.maximum(gap, 0)), 0) * HD ** -0.5
        c[:, C_KD + h] = np.exp(lg[h] * (P - 1 - i)) * HD ** -0.5
        rows = slice((h % 2) * HD, (h % 2 + 1) * HD)
        c[rows, C_QD + h // 2 * P:C_QD + (h // 2 + 1) * P] = np.exp(lg[h] * (i + 1))[None, :]
        c[rows, C_CD + h // 2] = np.exp(lg[h] * P)
    c[:, C_FREQ] = ROPE_BASE ** (-(i % (HD // 2)) / (HD // 2))
    c[:, C_SIGN] = np.where(i % HD < HD // 2, 1.0, -1.0)
    return c.astype(np.float32)


def wide(ap, n):
    return ap.unsqueeze(2).broadcast_to([ap.shape[0], ap.shape[1], n])


def build(nc, x, mem, positions, norm_g, w_in, w_out, mem_norm_g, w_mem_kv, mem_q_norm_g, mem_k_norm_g,
          ret_norm_g, consts, out):
    proj = nc.dram_tensor("proj", (NBLK * P, SEQ), F32, kind="Internal").ap()
    proj_lo = nc.dram_tensor("proj_lo", (RETQ * P, SEQ), F32, kind="Internal").ap()
    mixed = nc.dram_tensor("mixed", (MIXP * P, SEQ), F32, kind="Internal").ap()
    rotary = nc.dram_tensor("rotary", (2 * P, SEQ), F32, kind="Internal").ap()
    mem_k = nc.dram_tensor("mem_k", (DEPTH, P, MEMP * MEM_TOKENS), F32, kind="Internal").ap()
    mem_v = nc.dram_tensor("mem_v", (DEPTH, P, 2 * MEM_HEADS * HD), F32, kind="Internal").ap()
    x_in = x.rearrange("b s d -> (b s) d")
    x_run = out.rearrange("b s d -> (b s) d")

    with ExitStack() as ctx:
        cst = ctx.enter_context(nc.sbuf_tensor("cst", [P, C_ALL], F32))
        prologue(nc, cst, x_in, x_run, mem, positions, mem_norm_g, w_mem_kv, mem_q_norm_g, mem_k_norm_g,
                 consts, rotary, mem_k, mem_v)
        with nc.Fori(0, DEPTH) as layer:
            project(nc, cst, layer, x_run, norm_g, w_in, rotary, proj, proj_lo)
            mix(nc, cst, proj, proj_lo, mixed)
            emit(nc, cst, layer, proj, mixed, mem_k, mem_v, ret_norm_g, w_out, x_run)


class Phase:

    def __init__(self, nc, name):
        self.nc, self.name, self.sems = nc, name, []

    def __enter__(self):
        self.stack = ExitStack()
        self.inner = ExitStack()
        return self

    def sb(self, name, shape, dt=F32):
        return self.stack.enter_context(self.nc.sbuf_tensor(f"{self.name}_{name}", shape, dt))

    def ps(self, name, shape):
        return self.stack.enter_context(self.nc.psum_tensor(f"{self.name}_{name}", shape, F32))

    def sem(self, name):
        s = self.stack.enter_context(self.nc.semaphore(f"{self.name}_{name}"))
        self.sems.append(s)
        return s

    def block(self):
        return self.inner.enter_context(self.nc.Block())

    def __exit__(self, *e):
        self.inner.__exit__(*e)
        if e[0] is None:
            for s in self.sems:
                self.nc.sync.sem_clear(s)
            self.nc.all_engine_barrier()
        self.stack.__exit__(*e)



def prologue(nc, cst, x_in, x_run, mem, positions, mem_norm_g, w_mem_kv, gq, gk, consts, rotary, mem_k, mem_v):
    MT = MEM_TOKENS // P
    KV = 2 * MEM_HEADS * HD
    KW = MEM_HEADS * HD
    with Phase(nc, "pro") as ph:
        pos_i = ph.sb("pos_i", [P, SEQ], I32)
        ang = ph.sb("ang", [P, SEQ])
        turns = ph.sb("turns", [P, SEQ])
        rest = ph.sb("rest", [P, SEQ])
        table = ph.sb("table", [P, 2, SEQ])
        m_rows = ph.sb("m_rows", [P, MT, D_MODEL])
        junk = ph.sb("junk", [P, D_MODEL])
        var = ph.sb("var", [P, 16])
        y = ph.sb("y", [P, 16])
        t = ph.sb("t", [P, 16])
        m_cols = ph.sb("m_cols", [P, KC, MEM_TOKENS])
        m_g = ph.sb("m_g", [P, DEPTH, KC])
        mg_cols = ph.sb("mg_cols", [P, KC, MEM_TOKENS])
        w_kv = ph.sb("w_kv", [P, 2, KC, KV])
        qk_g = ph.sb("qk_g", [P, 2, DEPTH])
        g_all = ph.sb("g_all", [P, DEPTH])
        ksq = ph.sb("ksq", [P, MT, KW])
        kn = ph.sb("kn", [P, MT, KW])
        k_out = ph.sb("k_out", [P, MEMP, MEM_TOKENS])
        v_out = ph.sb("v_out", [P, MT, KW])
        ps_t = ph.ps("ps_t", [P, 4, 512])
        ps_kv = ph.ps("ps_kv", [P, MT, 512])
        ps_k = ph.ps("ps_k", [P, MEMP, MEM_TOKENS])

        cst_in, pos_in, mem_in, g_in = (ph.sem(n) for n in ("cst_in", "pos_in", "mem_in", "g_in"))
        w_loaded = [ph.sem(f"w_loaded{i}") for i in range(2)]
        x_copied, stored = ph.sem("x_copied"), ph.sem("stored")
        table_ready, table_stored = ph.sem("table_ready"), ph.sem("table_stored")
        sq_ready, root_ready, turned, kv_ready, k_turned = (
            ph.sem(n) for n in ("sq_ready", "root_ready", "turned", "kv_ready", "k_turned"))
        dve, act = ph.sem("dve"), ph.sem("act")
        var_ready, rows_ready, cols_ready, kn_ready, out_ready, ang_ready = (
            ph.sem(n) for n in ("var_ready", "rows_ready", "cols_ready", "kn_ready", "out_ready", "ang_ready"))
        block = ph.block()

        @block.sync
        def _(sp):
            sp.dma_start(cst[:, :], consts).then_inc(cst_in, 16)
            pos_rows = positions.broadcast_to([P, SEQ]) if positions.shape[0] == 1 else positions
            sp.dma_start(pos_i[:, :], pos_rows).then_inc(pos_in, 16)
            sp.dma_start(m_rows[:, :, :], mem[0].rearrange("(m p) d -> p m d", p=P)).then_inc(mem_in, 16)
            for l in range(DEPTH):
                sp.dma_start(m_g[:, l, :], mem_norm_g[l].rearrange("(c p) -> p c", p=P),
                             allow_slow_non_contiguous=True).then_inc(g_in, 16)
                for half in range(2):
                    for i, g in enumerate((gq, gk)):
                        sp.dma_start(qk_g[half * HD:(half + 1) * HD, i, l:l + 1],
                                     g[l].rearrange("(d o) -> d o", o=1)).then_inc(g_in, 16)
                sp.dma_start(w_kv[:, l, :, :], w_mem_kv[l].rearrange("(c p) n -> p c n", p=P)).then_inc(w_loaded[l], 16)
            for i in range(2):
                sp.wait_ge(table_ready, i + 1)
                sp.dma_start(rotary[i * P:(i + 1) * P, :], table[:, i, :]).then_inc(table_stored, 16)
            for l in range(DEPTH):
                sp.wait_ge(out_ready, 2 * l + 2)
                sp.dma_start(mem_k[l], k_out[:, :, :].rearrange("p a n -> p (a n)")).then_inc(stored, 16)
                sp.dma_start(mem_v[l], v_out[:, :, :].rearrange("p a n -> p (a n)")).then_inc(stored, 16)
            sp.wait_ge(table_stored, 32)
            sp.wait_ge(stored, 32 * DEPTH)
            sp.wait_ge(x_copied, 16 * 4)

        @block.gpsimd
        def _(pool):
            for i in range(4):
                rows = slice(i * SEQ // 4, (i + 1) * SEQ // 4)
                pool.dma_start(x_run[rows, :], x_in[rows, :]).then_inc(x_copied, 16)

        @block.scalar
        def _(act_e):
            act_e.wait_ge(mem_in, 16)
            for m in range(MT):
                if m:
                    act_e.wait_ge(sq_ready, m)
                nc.scalar.activation(junk[:, :], m_rows[:, m, :], ACT.Square, accum_out=var[:, m:m + 1]).then_inc(sq_ready, 1)
            act_e.wait_ge(var_ready, 1)
            nc.scalar.activation(t[:, 0:MT], var[:, 0:MT], ACT.Ln).then_inc(act, 1)
            act_e.wait_ge(act, 1)
            nc.scalar.activation(y[:, 0:MT], t[:, 0:MT], ACT.Exp, scale=-0.5).then_inc(root_ready, 1)
            act_e.wait_ge(ang_ready, 1)
            nc.scalar.activation(table[:, 0, :], rest[:, :], ACT.Sin).then_inc(table_ready, 1)
            act_e.wait_ge(ang_ready, 2)
            nc.scalar.activation(table[:, 1, :], turns[:, :], ACT.Sin, scale=cst[:, C_SIGN:C_SIGN + 1]).then_inc(table_ready, 1)
            for l in range(DEPTH):
                for m in range(MT):
                    act_e.wait_ge(kv_ready, MT * l + m + 1)
                    nc.scalar.activation(ksq[:, m, :], ps_kv[:, m, 0:KW], ACT.Square).then_inc(sq_ready, 1)
                act_e.wait_ge(var_ready, l + 2)
                nc.scalar.activation(t[:, 2:2 + MT * MEM_HEADS], var[:, 2:2 + MT * MEM_HEADS], ACT.Ln).then_inc(act, 1)
                act_e.wait_ge(act, l + 2)
                nc.scalar.activation(y[:, 2:2 + MT * MEM_HEADS], t[:, 2:2 + MT * MEM_HEADS], ACT.Exp, scale=-0.5).then_inc(root_ready, 1)

        @block.tensor
        def _(pe):
            pe.wait_ge(cst_in, 16)
            pe.wait_ge(rows_ready, MT)
            for c in range(KC):
                for m in range(MT):
                    k = c * MT + m
                    mm = nc.tensor.transpose(ps_t[:, k // 4, (k % 4) * P:(k % 4 + 1) * P], m_rows[:, m, c * P:(c + 1) * P],
                                             cst[:, C_ID:C_ID + P])
            mm.then_inc(turned, 1)
            for l in range(DEPTH):
                pe.wait_ge(cols_ready, l + 2)
                pe.wait_ge(w_loaded[l], 16)
                if l:
                    pe.wait_ge(out_ready, 2 * l)
                for m in range(MT):
                    for c in range(KC):
                        mm = nc.tensor.matmul(ps_kv[:, m, :], mg_cols[:, c, m * P:(m + 1) * P], w_kv[:, l, c, :],
                                              start=c == 0, stop=c == KC - 1)
                    mm.then_inc(kv_ready, 1)
                pe.wait_ge(kn_ready, l + 1)
                for p in range(MEMP):
                    for m in range(MT):
                        mm = nc.tensor.transpose(ps_k[:, p, m * P:(m + 1) * P], kn[:, m, p * P:(p + 1) * P],
                                                 cst[:, C_ID:C_ID + P])
                mm.then_inc(k_turned, 1)

        @block.vector
        def _(v):
            n = [0]

            def step(ins):
                n[0] += 1
                ins.then_inc(dve, 1)
                v.wait_ge(dve, n[0])

            def newton(a, b):
                step(nc.vector.tensor_tensor(t[:, a:b], y[:, a:b], y[:, a:b], ALU.mult))
                step(nc.vector.scalar_tensor_tensor(t[:, a:b], t[:, a:b], -0.5, var[:, a:b], ALU.mult, ALU.mult))
                step(nc.vector.scalar_tensor_tensor(y[:, a:b], t[:, a:b], 1.5, y[:, a:b], ALU.add, ALU.mult))

            v.wait_ge(sq_ready, MT)
            nc.vector.tensor_scalar(var[:, 0:MT], var[:, 0:MT], 1.0 / D_MODEL, EPS, ALU.mult, ALU.add).then_inc(var_ready, 1)
            v.wait_ge(var_ready, 1)
            v.wait_ge(root_ready, 1)
            newton(0, MT)
            for m in range(MT):
                nc.vector.tensor_scalar(m_rows[:, m, :], m_rows[:, m, :], y[:, m:m + 1], None, ALU.mult).then_inc(rows_ready, 1)
            v.wait_ge(cst_in, 16)
            v.wait_ge(pos_in, 16)
            step(nc.vector.tensor_copy(ang[:, :], pos_i[:, :]))
            step(nc.vector.tensor_scalar(ang[:, :], ang[:, :], cst[:, C_FREQ:C_FREQ + 1], None, ALU.mult))
            big = 1.5 * 2.0 ** 23
            c1, c2 = 6.28125, 0.0019340515136718750
            c3 = 2 * np.pi - c1 - c2
            for i, dst in ((0, rest), (1, turns)):
                step(nc.vector.tensor_scalar(turns[:, :], ang[:, :], float(1 / (2 * np.pi)), 0.25 if i == 0 else 0.0, ALU.mult, ALU.add))
                step(nc.vector.tensor_scalar(turns[:, :], turns[:, :], big, None, ALU.add))
                step(nc.vector.tensor_scalar(turns[:, :], turns[:, :], big, None, ALU.subtract))
                if i == 0:
                    step(nc.vector.scalar_tensor_tensor(rest[:, :], turns[:, :], -c1, ang[:, :], ALU.mult, ALU.add))
                    step(nc.vector.scalar_tensor_tensor(rest[:, :], turns[:, :], -c2, rest[:, :], ALU.mult, ALU.add))
                    step(nc.vector.scalar_tensor_tensor(rest[:, :], turns[:, :], -float(c3), rest[:, :], ALU.mult, ALU.add))
                    step(nc.vector.tensor_scalar(rest[:, :], rest[:, :], float(np.pi / 2), 3.1415925, ALU.add, ALU.min))
                    nc.vector.tensor_scalar(rest[:, :], rest[:, :], -3.1415925, None, ALU.max).then_inc(ang_ready, 1)
                else:
                    step(nc.vector.scalar_tensor_tensor(ang[:, :], turns[:, :], -c1, ang[:, :], ALU.mult, ALU.add))
                    step(nc.vector.scalar_tensor_tensor(ang[:, :], turns[:, :], -c2, ang[:, :], ALU.mult, ALU.add))
                    step(nc.vector.scalar_tensor_tensor(ang[:, :], turns[:, :], -float(c3), ang[:, :], ALU.mult, ALU.add))
                    nc.vector.tensor_scalar(turns[:, :], ang[:, :], -3.1415925, 3.1415925, ALU.max, ALU.min).then_inc(ang_ready, 1)
            v.wait_ge(turned, 1)
            for j in range(4):
                ins = nc.vector.tensor_copy(m_cols[:, 2 * j:2 * j + 2, :], ps_t[:, j, :].rearrange("p (a n) -> p a n", a=2))
            ins.then_inc(cols_ready, 1)
            v.wait_ge(cols_ready, 1)
            v.wait_ge(g_in, 16 * 5 * DEPTH)
            step(nc.vector.scalar_tensor_tensor(g_all[:, :], qk_g[:, 0, :], HD ** -0.5, qk_g[:, 1, :], ALU.mult, ALU.mult))
            a, b = 2, 2 + MT * MEM_HEADS
            for l in range(DEPTH):
                if l:
                    v.wait_ge(kv_ready, MT * l)
                nc.vector.tensor_tensor(mg_cols[:, :, :], m_cols[:, :, :], wide(m_g[:, l, :], MEM_TOKENS), ALU.mult).then_inc(cols_ready, 1)
                v.wait_ge(sq_ready, MT * (l + 2))
                step(nc.vector.tensor_reduce(var[:, a:b], ksq[:, :, :].rearrange("p m (h d) -> p (m h) d", d=HD), AX.X, ALU.add))
                nc.vector.tensor_scalar(var[:, a:b], var[:, a:b], 1.0 / HD, EPS, ALU.mult, ALU.add).then_inc(var_ready, 1)
                v.wait_ge(var_ready, l + 2)
                v.wait_ge(root_ready, l + 2)
                newton(a, b)
                if l:
                    v.wait_ge(stored, 32 * l)
                for m in range(MT):
                    ins = nc.vector.tensor_tensor(
                        kn[:, m, :].rearrange("p (h d) -> p h d", d=HD), ps_kv[:, m, 0:KW].rearrange("p (h d) -> p h d", d=HD),
                        wide(y[:, a + m * MEM_HEADS:a + (m + 1) * MEM_HEADS], HD), ALU.mult)
                ins.then_inc(kn_ready, 1)
                nc.vector.tensor_copy(v_out[:, :, :], ps_kv[:, :, KW:KV]).then_inc(out_ready, 1)
                v.wait_ge(k_turned, l + 1)
                nc.vector.tensor_scalar(k_out[:, :, :], ps_k[:, :, :], g_all[:, l:l + 1], None, ALU.mult).then_inc(out_ready, 1)



def project(nc, cst, layer, x_run, norm_g, w_in, rotary, proj, proj_lo):
    XR = 4
    PAIRS = NBLK // 2
    with Phase(nc, "prj") as ph:
        h_hi = ph.sb("h_hi", [P, KC, SEQ], F32R)
        h_lo = ph.sb("h_lo", [P, KC, SEQ], F32R)
        x_t = ph.sb("x_t", [P, XR, D_MODEL])
        table = x_t[:, :, :].rearrange("p (a b) n -> p a (b n)", a=2)
        junk = ph.sb("junk", [P, D_MODEL])
        hg = ph.sb("hg", [P, 2, KC, P])
        g_c = ph.sb("g_c", [P, KC])
        var, y, t, lv = (ph.sb(n, [P, TILES]) for n in ("var", "y", "t", "lv"))
        w_raw = ph.sb("w_raw", [P, 2, KC, P])
        w_hi = ph.sb("w_hi", [P, 2, KC, P], F32R)
        w_lo = ph.sb("w_lo", [P, 2, KC, P], F32R)
        stage = ph.sb("stage", [P, SPANS, SPAN])
        extra = ph.sb("extra", [P, SPANS, SPAN])
        ps_t = [ph.ps(f"ps_t{i}", [P, KC, P]) for i in range(2)]
        ps_a = [ph.ps(f"ps_a{i}", [P, SPAN]) for i in range(SPANS)]

        x_loaded = [ph.sem(f"x_loaded{i}") for i in range(XR)]
        w_loaded = [ph.sem(f"w_loaded{i}") for i in range(2)]
        g_loaded, table_loaded = ph.sem("g_loaded"), ph.sem("table_loaded")
        stored = [ph.sem(f"stored{c}") for c in range(SPANS)]
        lo_stored = [ph.sem(f"lo_stored{c}") for c in range(SPANS)]
        squared, var_ready, log_ready, root_ready, dve, x_scaled = (
            ph.sem(n) for n in ("squared", "var_ready", "log_ready", "root_ready", "dve", "x_scaled"))
        x_turned, hg_ready, hi_ready, lo_ready = (ph.sem(n) for n in ("x_turned", "hg_ready", "hi_ready", "lo_ready"))
        whi_ready, wlo_ready, acc_ready, evacuated, copied, sig_ready, rotated = (
            ph.sem(n) for n in ("whi_ready", "wlo_ready", "acc_ready", "evacuated", "copied", "sig_ready", "rotated"))
        block = ph.block()
        w_l = w_in[bass.ds(layer, 1)].rearrange("o (c p) n -> (o p) c n", p=P)

        def by_pairs(eng, body):
            for kind, n0, n1 in KINDS:
                lo, hi = n0 // 2, n1 // 2
                if lo == 0:
                    body(0, kind, False)
                    lo = 1
                if hi == PAIRS:
                    hi -= 1
                with eng.Fori(lo, hi) as pair:
                    body(pair, kind, False)
            body(PAIRS - 1, KINDS[-1][0], True)

        @block.sync
        def _(sp):
            def load_w(n):
                if n >= 2:
                    sp.wait_ge(whi_ready, n - 1)
                    sp.wait_ge(wlo_ready, n - 1)
                b = ORDER[n]
                sp.dma_start(w_raw[:, n % 2, :, :], w_l[:, :, b * P:(b + 1) * P]).then_inc(w_loaded[n % 2], 16)

            sp.dma_start(g_c[:, :], norm_g[bass.ds(layer, 1)].rearrange("o (c p) -> (o p) c", p=P),
                         allow_slow_non_contiguous=True).then_inc(g_loaded, 16)
            for i in range(TILES):
                if i >= XR:
                    sp.wait_ge(x_turned, i - XR + 1)
                sp.dma_start(x_t[:, i % XR, :], x_run[i * P:(i + 1) * P, :]).then_inc(x_loaded[i % XR], 16)
                if i in (0, 3):
                    load_w(i // 3)
            sp.wait_ge(x_turned, TILES)
            for i in range(2):
                sp.dma_start(table[:, i, :], rotary[i * P:(i + 1) * P, :]).then_inc(table_loaded, 16)
            for kind, n0, n1 in KINDS:
                for n in range(n0, n1):
                    if 2 <= n + 1 < NBLK:
                        load_w(n + 1)
                    for c in range(SPANS):
                        cols = slice(c * SPAN, (c + 1) * SPAN)
                        if kind == "rotate":
                            sp.wait_ge(rotated, SPANS * (n - RETQ) + c + 1)
                        else:
                            sp.wait_ge(evacuated, SPANS * n + c + 1)
                        sp.dma_start(proj[n * P:(n + 1) * P, cols], stage[:, c, :]).then_inc(stored[c], 16)
                        if kind == "split":
                            sp.dma_start(proj_lo[n * P:(n + 1) * P, cols], extra[:, c, :]).then_inc(lo_stored[c], 16)
            for c in range(SPANS):
                sp.wait_ge(stored[c], 16 * NBLK)
                sp.wait_ge(lo_stored[c], 16 * RETQ)

        @block.scalar
        def _(act):
            def w_split(pair, slot):
                act.wait_ge(w_loaded[slot], (pair + 1) * 16)
                if not (isinstance(pair, int) and pair == 0):
                    act.wait_ge(acc_ready, (2 * pair + slot - 1) * SPANS)
                nc.scalar.copy(w_hi[:, slot, :, :], w_raw[:, slot, :, :]).then_inc(whi_ready, 1)

            def stage_free(n, c):
                if not (isinstance(n, int) and n == 0):
                    act.wait_ge(stored[c], n * 16)

            def blocks(pair, kind, last):
                for slot in range(2):
                    n = 2 * pair + slot
                    for c in range(SPANS):
                        if kind == "split":
                            act.wait_ge(acc_ready, n * SPANS + c + 1)
                            stage_free(n, c)
                            nc.scalar.copy(stage[:, c, :].bitcast(F32R), ps_a[c][:, :]).then_inc(copied, 1)
                        if kind == "gate":
                            act.wait_ge(acc_ready, n * SPANS + c + 1)
                            stage_free(n, c)
                            nc.scalar.activation(stage[:, c, :], ps_a[c][:, :], ACT.Sigmoid).then_inc(sig_ready, 1)
                        if c == 0 and not (last and slot == 1):
                            w_split(pair + slot, 1 - slot)

            nc.scalar.preload_act_table_set("natural_log_exp_and_others")
            for i in range(TILES + 3):
                if i < TILES:
                    act.wait_ge(x_loaded[i % XR], 16 * (i // XR + 1))
                    if i:
                        act.wait_ge(squared, i)
                    nc.scalar.activation(junk[:, :], x_t[:, i % XR, :], ACT.Square, accum_out=var[:, i:i + 1]).then_inc(squared, 1)
                if 0 <= i - 1 < TILES:
                    j = i - 1
                    act.wait_ge(var_ready, j + 1)
                    nc.scalar.activation(lv[:, j:j + 1], var[:, j:j + 1], ACT.Ln).then_inc(log_ready, 1)
                    act.wait_ge(log_ready, j + 1)
                    nc.scalar.activation(y[:, j:j + 1], lv[:, j:j + 1], ACT.Exp, scale=-0.5).then_inc(root_ready, 1)
                if 0 <= i - 3 < TILES:
                    j = i - 3
                    act.wait_ge(hg_ready, j + 1)
                    nc.scalar.copy(h_hi[:, :, j * P:(j + 1) * P], hg[:, j % 2, :, :]).then_inc(hi_ready, 1)
                if i == 1:
                    w_split(0, 0)
            by_pairs(act, blocks)

        @block.gpsimd
        def _(pool):
            def w_split(pair, slot):
                n = 2 * pair + slot
                pool.wait_ge(whi_ready, n + 1)
                if not (isinstance(pair, int) and pair == 0):
                    pool.wait_ge(acc_ready, (n - 1) * SPANS)
                nc.gpsimd.tensor_tensor(w_lo[:, slot, :, :], w_raw[:, slot, :, :], w_hi[:, slot, :, :], ALU.subtract).then_inc(wlo_ready, 1)

            def blocks(pair, kind, last):
                for slot in range(2):
                    n = 2 * pair + slot
                    if not (last and slot == 1):
                        w_split(pair + slot, 1 - slot)
                    if kind == "rotate":
                        for c in range(SPANS):
                            pool.wait_ge(evacuated, n * SPANS + c + 1)
                            nc.gpsimd.tensor_tensor(stage[:, c, :], stage[:, c, :], extra[:, c, :], ALU.add).then_inc(rotated, 1)

            for j in range(TILES):
                pool.wait_ge(hi_ready, j + 1)
                nc.gpsimd.tensor_tensor(h_lo[:, :, j * P:(j + 1) * P], hg[:, j % 2, :, :], h_hi[:, :, j * P:(j + 1) * P],
                                        ALU.subtract).then_inc(lo_ready, 1)
                if j == 0:
                    w_split(0, 0)
            by_pairs(pool, blocks)

        @block.vector
        def _(v):
            n_dve = [0]

            def step(ins):
                n_dve[0] += 1
                ins.then_inc(dve, 1)
                v.wait_ge(dve, n_dve[0])

            def blocks(pair, kind, last):
                for slot in range(2):
                    n = 2 * pair + slot
                    first = isinstance(pair, int) and n == 0
                    for c in range(SPANS):
                        a, to, other = ps_a[c], stage[:, c, :], extra[:, c, :]
                        if kind == "split":
                            v.wait_ge(copied, n * SPANS + c + 1)
                            if not first:
                                v.wait_ge(lo_stored[c], n * 16)
                            nc.vector.tensor_tensor(other.bitcast(F32R), a[:, :], to.bitcast(F32R), ALU.subtract).then_inc(evacuated, 1)
                        elif kind == "rotate":
                            cols = slice(c * SPAN, (c + 1) * SPAN)
                            v.wait_ge(acc_ready, n * SPANS + c + 1)
                            v.wait_ge(table_loaded, 32)
                            v.wait_ge(stored[c], n * 16)
                            v.wait_ge(lo_stored[c], 16 * RETQ)
                            nc.vector.tensor_tensor(to, a[:, :], table[:, 0, cols], ALU.mult)
                            for q in range(4):
                                src, dst = slice((q ^ 1) * 32, (q ^ 1) * 32 + 32), slice(q * 32, q * 32 + 32)
                                ins = nc.vector.tensor_tensor(extra[dst, c, :], a[src, :], table[src, 1, cols], ALU.mult)
                            ins.then_inc(evacuated, 1)
                        elif kind == "plain":
                            v.wait_ge(acc_ready, n * SPANS + c + 1)
                            v.wait_ge(stored[c], n * 16)
                            nc.vector.tensor_copy(to, a[:, :]).then_inc(evacuated, 1)
                        else:
                            v.wait_ge(sig_ready, (n - GATE0) * SPANS + c + 1)
                            nc.vector.tensor_tensor(to, a[:, :], to, ALU.mult).then_inc(evacuated, 1)

            v.wait_ge(g_loaded, 16)
            for i in range(TILES + 2):
                if i < TILES:
                    v.wait_ge(squared, i + 1)
                    nc.vector.tensor_scalar(var[:, i:i + 1], var[:, i:i + 1], 1.0 / D_MODEL, EPS, ALU.mult, ALU.add).then_inc(var_ready, 1)
                if 0 <= i - 1 < TILES:
                    j = i - 1
                    v.wait_ge(root_ready, j + 1)
                    v.wait_ge(var_ready, j + 1)
                    s = slice(j, j + 1)
                    step(nc.vector.tensor_tensor(t[:, s], y[:, s], y[:, s], ALU.mult))
                    step(nc.vector.scalar_tensor_tensor(t[:, s], t[:, s], -0.5, var[:, s], ALU.mult, ALU.mult))
                    step(nc.vector.scalar_tensor_tensor(y[:, s], t[:, s], 1.5, y[:, s], ALU.add, ALU.mult))
                    nc.vector.tensor_scalar(x_t[:, j % XR, :], x_t[:, j % XR, :], y[:, s], None, ALU.mult).then_inc(x_scaled, 1)
                if 0 <= i - 2 < TILES:
                    j = i - 2
                    v.wait_ge(x_turned, j + 1)
                    if j >= 2:
                        v.wait_ge(lo_ready, j - 1)
                    nc.vector.tensor_tensor(hg[:, j % 2, :, :], ps_t[j % 2][:, :, :], wide(g_c[:, :], P), ALU.mult).then_inc(hg_ready, 1)
            by_pairs(v, blocks)

        @block.tensor
        def _(pe):
            def turn(j):
                pe.wait_ge(x_scaled, j + 1)
                if j >= 2:
                    pe.wait_ge(hg_ready, j - 1)
                for k in range(KC):
                    mm = nc.tensor.transpose(ps_t[j % 2][:, k, :], x_t[:, j % XR, k * P:(k + 1) * P], cst[:, C_ID:C_ID + P])
                mm.then_inc(x_turned, 1)

            def matmuls(slot, c):
                for k in range(KC):
                    for i, (w, h) in enumerate(((w_hi, h_hi), (w_hi, h_lo), (w_lo, h_hi))):
                        mm = nc.tensor.matmul(ps_a[c][:, :], w[:, slot, k, :], h[:, k, c * SPAN:(c + 1) * SPAN],
                                              start=k == 0 and i == 0, stop=k == KC - 1 and i == 2)
                mm.then_inc(acc_ready, 1)

            for j in range(TILES // 2):
                turn(j)
            pe.wait_ge(whi_ready, 1)
            pe.wait_ge(wlo_ready, 1)
            for c in range(SPANS):
                pe.wait_ge(hi_ready, 4 * c + 4)
                pe.wait_ge(lo_ready, 4 * c + 4)
                matmuls(0, c)
                for j in range(TILES // 2 + 4 * c, min(TILES // 2 + 4 * c + 4, TILES)):
                    turn(j)
            pe.wait_ge(whi_ready, 2)
            pe.wait_ge(wlo_ready, 2)
            for c in range(SPANS):
                pe.wait_ge(evacuated, c + 1)
                matmuls(1, c)
            with pe.Fori(1, PAIRS) as pair:
                for slot in range(2):
                    pe.wait_ge(whi_ready, 2 * pair + slot + 1)
                    pe.wait_ge(wlo_ready, 2 * pair + slot + 1)
                    for c in range(SPANS):
                        pe.wait_ge(evacuated, (2 * pair + slot - 1) * SPANS + c + 1)
                        matmuls(slot, c)



class Unit:

    def __init__(self, n, t, h, lo, width, first, last):
        self.n, self.t, self.h, self.lo, self.width, self.first, self.last = n, t, h, lo, width, first, last
        self.row = t * SB_HEADS + h


def units():
    found = []
    for t in range(TILES):
        count = -(-(t + 1) * P // SPAN)
        cuts = [(t + 1) * u // count * P for u in range(count + 1)]
        for h in range(SB_HEADS):
            for u in range(count - 1, -1, -1):
                found.append(Unit(len(found), t, h, cuts[u], cuts[u + 1] - cuts[u], u == count - 1, u == 0))
    return found


def mix(nc, cst, proj, proj_lo, mixed):
    U = units()
    first = [next(u.n for u in U if u.t == t) for t in range(TILES)] + [len(U)]
    SIDE = ("turn_v", "", "", "", "turn_k", "turn_rv", "", "", "", "scores1", "scores2", "", "", "", "out0", "", "out1", "",
            "out2", "", "kv", "", "", "")
    side = {}
    for t in range(TILES):
        n = first[t + 1] - first[t]
        for k, what in enumerate(SIDE):
            if what:
                side.setdefault(first[t] + k * n // len(SIDE), []).append((what, t + 1 if what == "turn_v" else t))
    B, W3 = 4, 3
    SIG, SCAN, WEIGH, TURN, SPLIT, PV, FOLD = range(1, 8)
    STEPS = len(U) + FOLD

    def at(n, stage):
        return (n - stage,) if 0 <= n - stage < len(U) else ()

    with Phase(nc, "mix") as ph:
        k_st = ph.sb("k_st", [P, SB_HEADS, SEQ], F32R)
        v_st = ph.sb("v_st", [P, TILES, SB_HEADS, 2, HD], F32R)
        v_in = ph.sb("v_in", [P, 2, SBP, P])
        r_in = ph.sb("r_in", [P, 2, 3 * RETP, P])
        q_hi = ph.sb("q_hi", [P, 2, SB_HEADS, P], F32R)
        q_lo = ph.sb("q_lo", [P, 2, SB_HEADS, P], F32R)
        eye = ph.sb("eye", [P, P], F32R)
        mask = ph.sb("mask", [P, P], F32R)
        beta = ph.sb("beta", [P, B, SPAN])
        keep = ph.sb("keep", [P, B, SPAN])
        stick = ph.sb("stick", [P, B, SPAN + 1])
        zero = ph.sb("zero", [P, SPAN])
        w_t = ph.sb("w_t", [P, W3, SPAN])
        wt = ph.sb("wt", [P, W3, SPAN // P, 2, P], F32R)
        f1 = ph.sb("f1", [HD, 2, 2 * P])
        f2 = ph.sb("f2", [HD, 2, 2 * P])
        o_t = ph.sb("o_t", [P, 2, MIXP, P])
        q_bd = ph.sb("q_bd", [P, 2, RETP, 2 * P])
        q_dec = ph.sb("q_dec", [P, RETP, P])
        k_hat = ph.sb("k_hat", [P, RETP * P])
        r_v = ph.sb("r_v", [P, RETP * P])
        sc = ph.sb("sc", [P, RET_HEADS, P])
        state = ph.sb("state", [P, RETP, P])
        ps_z = [ph.ps(f"ps_z{i}", [P, SPAN]) for i in range(2)]
        ps_w = [ph.ps(f"ps_w{i}", [P, SPAN]) for i in range(2)]
        ps_o = [ph.ps(f"ps_o{i}", [P, 512]) for i in range(2)]
        ps_1 = ph.ps("ps_1", [P, 512])
        ps_2 = ph.ps("ps_2", [P, 512])

        names = ("consts_ready z_ready sig_ready scanned seeded weighted w_turned wt_hi wt_lo pv_ready folded1 folded2 "
                 "folded zeroed qdec_ready "
                 "v_turned v_hi v_lo k_turned rv_turned khat_ready rv_ready scores1_ready scores2_ready sc_ready out_ready "
                 "ret_copied kv_ready "
                 "state_decayed state_ready").split()
        s = {n: ph.sem(n) for n in names}
        (consts_ready, z_ready, sig_ready, scanned, seeded, weighted, w_turned, wt_hi, wt_lo, pv_ready, folded1, folded2,
         folded, zeroed, qdec_ready,
         v_turned, v_hi, v_lo, k_turned, rv_turned, khat_ready, rv_ready, scores1_ready, scores2_ready, sc_ready, out_ready,
         ret_copied, kv_ready,
         state_decayed, state_ready) = (s[n] for n in names)
        sb_loaded = [ph.sem(f"sb_loaded{i}") for i in range(2)]
        ret_loaded = [ph.sem(f"ret_loaded{i}") for i in range(2)]
        o_stored = [ph.sem(f"o_stored{i}") for i in range(2)]
        v_loaded = [ph.sem(f"v_loaded{i}") for i in range(2)]
        SB_DMAS, RET_DMAS = 6, 4
        block = ph.block()

        @block.sync
        def _(sp):
            his = proj[0:RETQ * P, :].rearrange("(h d) n -> d h n", d=HD)
            los = proj_lo.rearrange("(h d) n -> d h n", d=HD)
            values = proj[SBV * P:RETV * P, :].rearrange("(b p) n -> p b n", p=P)
            ret_qk = proj[RETQ * P:SBV * P, :].rearrange("(b p) n -> p b n", p=P)
            ret_q = proj[RETQ * P:(RETQ + RETP) * P, :].rearrange("(b i d) n -> i d b n", i=2, d=HD)
            ret_v = proj[RETV * P:MEMQ * P, :].rearrange("(b p) n -> p b n", p=P)
            to = mixed.rearrange("(b p) n -> p b n", p=P)

            def load(t):
                at, cols = t % 2, slice(t * P, (t + 1) * P)
                for half, of in enumerate((his, los)):
                    rows = slice(half * HD, (half + 1) * HD)
                    sp.dma_start(k_st[rows, :, cols].bitcast(F32), of[:, SB_HEADS:2 * SB_HEADS, cols]).then_inc(sb_loaded[at], 16)
                if t >= 2:
                    sp.wait_ge(z_ready, first[t - 1])
                for q, of in ((q_hi, his), (q_lo, los)):
                    for half in range(2):
                        rows = slice(half * HD, (half + 1) * HD)
                        sp.dma_start(q[rows, at, :, :].bitcast(F32), of[:, 0:SB_HEADS, cols]).then_inc(sb_loaded[at], 16)
                if t >= 2:
                    sp.wait_ge(v_turned, t - 1)
                sp.dma_start(v_in[:, at, :, :], values[:, :, cols]).then_inc(v_loaded[at], 16)
                if t >= 2:
                    sp.wait_ge(scores2_ready, t - 1)
                    sp.wait_ge(qdec_ready, t - 1)
                else:
                    sp.wait_ge(zeroed, 1)
                for i in range(2):
                    rows, at_cols = slice(i * HD, (i + 1) * HD), slice(i * P, (i + 1) * P)
                    sp.dma_start(q_bd[rows, at, :, at_cols], ret_q[i, :, :, cols]).then_inc(ret_loaded[at], 16)
                sp.dma_start(r_in[:, at, 0:2 * RETP, :], ret_qk[:, :, cols]).then_inc(ret_loaded[at], 16)
                sp.dma_start(r_in[:, at, 2 * RETP:3 * RETP, :], ret_v[:, :, cols]).then_inc(ret_loaded[at], 16)

            load(0)
            load(1)
            for t in range(TILES):
                if t + 2 < TILES:
                    load(t + 2)
                sp.wait_ge(folded, SB_HEADS * (t + 1))
                sp.wait_ge(ret_copied, t + 1)
                sp.dma_start(to[:, :, t * P:(t + 1) * P], o_t[:, t % 2, :, :]).then_inc(o_stored[t % 2], 16)
            for i in range(2):
                sp.wait_ge(o_stored[i], 16 * TILES // 2)

        @block.tensor
        def _(pe):
            def turn_v(t):
                if t >= TILES:
                    return
                pe.wait_ge(v_loaded[t % 2], 16 * (t // 2 + 1))
                if t == 1:
                    pe.wait_ge(v_lo, 1)
                if t >= 2:
                    pe.wait_ge(ret_copied, t - 1)
                for p in range(SBP):
                    mm = nc.tensor.transpose(ps_1[:, p * P:(p + 1) * P], v_in[:, t % 2, p, :], cst[:, C_ID:C_ID + P])
                mm.then_inc(v_turned, 1)

            def turn_k(t):
                pe.wait_ge(ret_loaded[t % 2], 16 * RET_DMAS * (t // 2 + 1))
                pe.wait_ge(v_lo, min(t + 2, TILES))
                pe.wait_ge(v_hi, min(t + 2, TILES))
                if t == TILES - 1:
                    pe.wait_ge(ret_copied, t)
                for p in range(RETP):
                    mm = nc.tensor.transpose(ps_1[:, p * P:(p + 1) * P], r_in[:, t % 2, RETP + p, :], cst[:, C_ID:C_ID + P])
                mm.then_inc(k_turned, 1)

            def turn_rv(t):
                if t >= 1:
                    pe.wait_ge(state_ready, t)
                for p in range(RETP):
                    mm = nc.tensor.transpose(ps_2[:, p * P:(p + 1) * P], r_in[:, t % 2, 2 * RETP + p, :], cst[:, C_ID:C_ID + P])
                mm.then_inc(rv_turned, 1)

            def scores1(t):
                pe.wait_ge(khat_ready, t + 1)
                for p in range(2):
                    mm = nc.tensor.matmul(ps_1[:, p * 2 * P:(p + 1) * 2 * P], r_in[:, t % 2, RETP + p, :], q_bd[:, t % 2, p, :],
                                          start=True, stop=True)
                mm.then_inc(scores1_ready, 1)

            def scores2(t):
                pe.wait_ge(rv_ready, t + 1)
                nc.tensor.matmul(ps_2[:, 0:2 * P], r_in[:, t % 2, RETP + 2, :], q_bd[:, t % 2, 2, :],
                                 start=True, stop=True).then_inc(scores2_ready, 1)

            def ret_out(p):
                def out(t):
                    pe.wait_ge(sc_ready, 2 * t + 2)
                    pe.wait_ge(qdec_ready, t + 1)
                    cols = slice(p * P, (p + 1) * P)
                    if t:
                        nc.tensor.matmul(ps_1[:, cols], state[:, p, :], q_dec[:, p, :], start=True, stop=False, skip_group_check=True)
                    for i in range(2):
                        rows = slice(i * HD, (i + 1) * HD)
                        mm = nc.tensor.matmul(ps_1[rows, cols], r_v[:, p * P + i * HD:p * P + (i + 1) * HD], sc[:, 2 * p + i, :],
                                              start=not t, stop=True, skip_group_check=True)
                    if p == RETP - 1:
                        mm.then_inc(out_ready, 1)
                return out

            def kv(t):
                for p in range(RETP):
                    cols = slice(p * P, (p + 1) * P)
                    mm = nc.tensor.matmul(ps_2[:, cols], k_hat[:, cols], r_v[:, cols], start=True, stop=True)
                mm.then_inc(kv_ready, 1)

            jobs = {"turn_v": turn_v, "turn_k": turn_k, "turn_rv": turn_rv, "scores1": scores1, "scores2": scores2,
                    "out0": ret_out(0), "out1": ret_out(1), "out2": ret_out(2), "kv": kv}
            pe.wait_ge(consts_ready, 4)
            turn_v(0)
            for n in range(STEPS):
                for m in at(n, TURN):
                    pe.wait_ge(weighted, m + 1)
                    if m >= 2:
                        pe.wait_ge(wt_lo, m - 1)
                    for b in range(U[m].width // P):
                        mm = nc.tensor.transpose(ps_w[m % 2][:, b * P:(b + 1) * P], w_t[:, m % W3, b * P:(b + 1) * P], cst[:, C_ID:C_ID + P])
                    mm.then_inc(w_turned, 1)
                for m in at(n, 0):
                    u = U[m]
                    if m == first[u.t]:
                        pe.wait_ge(sb_loaded[u.t % 2], 16 * SB_DMAS * (u.t // 2 + 1))
                    if m >= 2:
                        pe.wait_ge(sig_ready, m - 1)
                    z, keys = ps_z[m % 2][:, 0:u.width], k_st[:, u.h, u.lo:u.lo + u.width]
                    nc.tensor.matmul(z, q_hi[:, u.t % 2, u.h, :], keys, start=True, stop=False)
                    mm = nc.tensor.matmul(z, q_lo[:, u.t % 2, u.h, :], keys, start=False, stop=not u.first)
                    if u.first:
                        mm = nc.tensor.matmul(ps_z[m % 2][:, u.width - P:u.width], eye[:, :], mask[:, :], start=False, stop=True)
                    mm.then_inc(z_ready, 1)
                for m in at(n, PV):
                    u = U[m]
                    pe.wait_ge(wt_lo, m + 1)
                    if u.first and u.h == 0:
                        pe.wait_ge(v_hi, u.t + 1)
                        pe.wait_ge(v_lo, u.t + 1)
                    if u.first and u.row >= 2:
                        pe.wait_ge(folded2, u.row - 1)
                    for b in range(u.width // P):
                        mm = nc.tensor.matmul(ps_o[u.row % 2][:, 0:2 * P],
                                              v_st[:, u.lo // P + b, u.h, :, :].rearrange("p a d -> p (a d)"),
                                              wt[:, m % W3, b, :, :].rearrange("p a q -> p (a q)"),
                                              start=u.first and b == 0, stop=u.last and b == u.width // P - 1)
                    mm.then_inc(pv_ready, 1)
                for what, t in side.get(n, ()):
                    jobs[what](t)

        @block.scalar
        def _(act):
            def turn_v(t):
                if t >= TILES:
                    return
                act.wait_ge(v_turned, t + 1)
                nc.scalar.copy(v_st[:, t, :, 0, :], ps_1[:, 0:SBP * P].rearrange("p (h d) -> p h d", d=HD)).then_inc(v_hi, 1)

            def copy_rv(t):
                act.wait_ge(rv_turned, t + 1)
                if t:
                    act.wait_ge(kv_ready, t)
                nc.scalar.copy(r_v[:, :], ps_2[:, 0:RETP * P]).then_inc(rv_ready, 1)

            def ret_out(t):
                act.wait_ge(out_ready, t + 1)
                if t >= 2:
                    act.wait_ge(o_stored[t % 2], 16 * (t // 2))
                nc.scalar.copy(o_t[:, t % 2, SBP:MIXP, :], ps_1[:, 0:RETP * P].rearrange("p (b n) -> p b n", n=P)).then_inc(ret_copied, 1)

            jobs = {"turn_v": turn_v, "turn_rv": copy_rv, "out2": ret_out}
            turn_v(0)
            for n in range(STEPS + 1):
                for m in at(n, SPLIT):
                    act.wait_ge(w_turned, m + 1)
                    if m >= W3:
                        act.wait_ge(pv_ready, m - W3 + 1)
                    blocks = U[m].width // P
                    nc.scalar.copy(wt[:, m % W3, 0:blocks, 0, :], ps_w[m % 2][:, 0:U[m].width].rearrange("p (b n) -> p b n", n=P)).then_inc(wt_hi, 1)
                for m in at(n, FOLD):
                    if U[m].last:
                        r = U[m].row
                        act.wait_ge(pv_ready, m + 1)
                        if r >= 2:
                            act.wait_ge(folded2, r - 1)
                        nc.scalar.copy(f1[:, r % 2, :], ps_o[r % 2][HD:P, 0:2 * P]).then_inc(folded1, 1)
                for m in at(n, SIG):
                    act.wait_ge(z_ready, m + 1)
                    if m >= B:
                        act.wait_ge(weighted, m - B + 1)
                        act.wait_ge(scanned, m - B + 1)
                    z = ps_z[m % 2][:, 0:U[m].width]
                    nc.scalar.activation(keep[:, m % B, 0:U[m].width], z, ACT.Sigmoid, scale=-HD ** -0.5)
                    nc.scalar.activation(beta[:, m % B, 0:U[m].width], z, ACT.Sigmoid, scale=HD ** -0.5).then_inc(sig_ready, 1)
                for what, t in side.get(n - 1, ()):
                    if what in jobs:
                        jobs[what](t)

        @block.vector
        def _(v):
            def turn_v(t):
                if t >= TILES:
                    return
                v.wait_ge(v_hi, t + 1)
                nc.vector.tensor_tensor(v_st[:, t, :, 1, :], ps_1[:, 0:SBP * P].rearrange("p (h d) -> p h d", d=HD),
                                        v_st[:, t, :, 0, :], ALU.subtract).then_inc(v_lo, 1)

            def decay_k(t):
                v.wait_ge(k_turned, t + 1)
                if t:
                    v.wait_ge(kv_ready, t)
                nc.vector.tensor_tensor(k_hat[:, :].rearrange("p (h d) -> p h d", d=HD),
                                        ps_1[:, 0:RETP * P].rearrange("p (h d) -> p h d", d=HD),
                                        wide(cst[:, C_KD:C_KD + RET_HEADS], HD), ALU.mult).then_inc(khat_ready, 1)

            dec = cst[:, C_DEC:C_QD].rearrange("p (h n) -> p h n", n=P)

            def decay_scores1(t):
                v.wait_ge(scores1_ready, t + 1)
                if t:
                    v.wait_ge(out_ready, t)
                nc.vector.tensor_tensor(sc[:, 0:4, :], ps_1[:, :].rearrange("p (h n) -> p h n", n=P), dec[:, 0:4, :],
                                        ALU.mult).then_inc(sc_ready, 1)

            def decay_scores2(t):
                v.wait_ge(scores2_ready, t + 1)
                nc.vector.tensor_tensor(sc[:, 4:6, :], ps_2[:, 0:2 * P].rearrange("p (h n) -> p h n", n=P), dec[:, 4:6, :],
                                        ALU.mult).then_inc(sc_ready, 1)

            def add_state(t):
                v.wait_ge(kv_ready, t + 1)
                v.wait_ge(state_decayed, t + 1)
                for i in range(2):
                    rows, cols = slice(i * HD, (i + 1) * HD), slice(i * HD, (i + 1) * HD)
                    ins = nc.vector.tensor_tensor(state[rows, :, cols], ps_2[rows, 0:RETP * P].rearrange("p (b n) -> p b n", n=P)[:, :, cols],
                                                  state[rows, :, cols], ALU.add)
                ins.then_inc(state_ready, 1)

            jobs = {"turn_v": turn_v, "turn_k": decay_k, "scores1": decay_scores1, "scores2": decay_scores2, "kv": add_state}
            nc.vector.memset(zero[:, :], 0.0).then_inc(consts_ready, 1)
            nc.vector.tensor_copy(eye[:, :], cst[:, C_ID:C_ID + P]).then_inc(consts_ready, 1)
            nc.vector.tensor_copy(mask[:, :], cst[:, C_MASK:C_MASK + P]).then_inc(consts_ready, 1)
            nc.vector.memset(state[:, :, :], 0.0).then_inc(consts_ready, 1)
            v.wait_ge(consts_ready, 4)
            turn_v(0)
            for n in range(STEPS + 1):
                for m in at(n, SCAN):
                    u = U[m]
                    slot, w = m % B, u.width
                    if m >= B:
                        v.wait_ge(weighted, m - B + 1)
                    end = stick[:, slot, w:w + 1]
                    if u.first:
                        nc.vector.memset(end, 1.0).then_inc(seeded, 1)
                        start = 1.0
                    else:
                        v.wait_ge(scanned, m)
                        start = stick[:, (m - 1) % B, 0:1]
                        nc.vector.tensor_copy(end, start).then_inc(seeded, 1)
                    v.wait_ge(sig_ready, m + 1)
                    nc.vector.tensor_tensor_scan(stick[:, slot, 0:w][:, ::-1], keep[:, slot, 0:w][:, ::-1], zero[:, 0:w], start,
                                                 ALU.mult, ALU.add).then_inc(scanned, 1)
                for m in at(n, SPLIT):
                    w = U[m].width
                    v.wait_ge(wt_hi, m + 1)
                    if m >= W3:
                        v.wait_ge(pv_ready, m - W3 + 1)
                    nc.vector.tensor_tensor(wt[:, m % W3, 0:w // P, 1, :], ps_w[m % 2][:, 0:w].rearrange("p (b n) -> p b n", n=P),
                                            wt[:, m % W3, 0:w // P, 0, :], ALU.subtract).then_inc(wt_lo, 1)
                for what, t in side.get(n - 1, ()):
                    if what in jobs:
                        jobs[what](t)
                for m in at(n, FOLD):
                    if U[m].last:
                        u = U[m]
                        r, slot = u.row, u.row % 2
                        v.wait_ge(folded1, r + 1)
                        if r >= 2:
                            v.wait_ge(folded, r - 1)
                        nc.vector.tensor_tensor(f2[:, slot, :], ps_o[slot][0:HD, 0:2 * P], f1[:, slot, :], ALU.add).then_inc(folded2, 1)
                        v.wait_ge(folded2, r + 1)
                        if u.t >= 2 and u.h == 0:
                            v.wait_ge(o_stored[u.t % 2], 16 * (u.t // 2))
                        rows = slice((u.h % 2) * HD, (u.h % 2 + 1) * HD)
                        nc.vector.tensor_tensor(o_t[rows, u.t % 2, u.h // 2, :], f2[:, slot, 0:P], f2[:, slot, P:2 * P], ALU.add).then_inc(folded, 1)

        @block.gpsimd
        def _(pool):
            def decay_q(t):
                pool.wait_ge(ret_loaded[t % 2], 16 * RET_DMAS * (t // 2 + 1))
                if t:
                    pool.wait_ge(out_ready, t)
                nc.gpsimd.tensor_tensor(q_dec[:, :, :], r_in[:, t % 2, 0:RETP, :], cst[:, C_QD:C_KD].rearrange("p (b n) -> p b n", n=P),
                                        ALU.mult).then_inc(qdec_ready, 1)

            def decay_state(t):
                pool.wait_ge(out_ready, t + 1)
                if t:
                    pool.wait_ge(state_ready, t)
                nc.gpsimd.tensor_tensor(state[:, :, :], state[:, :, :], wide(cst[:, C_CD:C_CD + RETP], P), ALU.mult).then_inc(state_decayed, 1)

            jobs = {"turn_k": decay_q, "out2": decay_state}
            nc.gpsimd.memset(q_bd[:, :, :, :], 0.0).then_inc(zeroed, 1)
            pool.wait_ge(consts_ready, 4)
            for n in range(STEPS + 1):
                for m in at(n, WEIGH):
                    w = U[m].width
                    pool.wait_ge(scanned, m + 1)
                    pool.wait_ge(seeded, m + 1)
                    if m >= W3:
                        pool.wait_ge(w_turned, m - W3 + 1)
                    nc.gpsimd.tensor_tensor(w_t[:, m % W3, 0:w], beta[:, m % B, 0:w], stick[:, m % B, 1:w + 1], ALU.mult).then_inc(weighted, 1)
                for what, t in side.get(n - 1, ()):
                    if what in jobs:
                        jobs[what](t)



def emit(nc, cst, layer, proj, mixed, mem_k, mem_v, ret_norm_g, w_out, x_run):
    MT = MEM_TOKENS // P
    R, XR = 4, 3
    NR = RETP * P
    NVAR = NR + MEM_HEADS
    with Phase(nc, "emt") as ph:
        wo_raw = ph.sb("wo_raw", [P, ALLP, D_MODEL])
        wo_hi = ph.sb("wo_hi", [P, ALLP, D_MODEL], F32R)
        wo_lo = ph.sb("wo_lo", [P, ALLP, D_MODEL], F32R)
        k_raw = ph.sb("k_raw", [P, MEMP, MEM_TOKENS])
        kb_raw = ph.sb("kb_raw", [P, MEMP, 2, MEM_TOKENS])
        kb_hi = ph.sb("kb_hi", [P, MEMP, 2 * MEM_TOKENS], F32R)
        kb_lo = ph.sb("kb_lo", [P, MEMP, 2 * MEM_TOKENS], F32R)
        m_v = ph.sb("m_v", [P, MT, MEM_HEADS * HD])
        r_g = ph.sb("r_g", [P, RETP])
        m = ph.sb("m", [P, R, ALLP, P])
        g = ph.sb("g", [P, R, ALLP, P])
        x_t = ph.sb("x_t", [P, XR, D_MODEL])
        sq = ph.sb("sq", [P, RETP + MEMP, P])
        var, tmp = (ph.sb(n, [P, NVAR]) for n in ("var", "tmp"))
        root = ph.sb("root", [P, 2, NVAR])
        q_hi = ph.sb("q_hi", [P, 2, MEMP, P], F32R)
        q_lo = ph.sb("q_lo", [P, 2, MEMP, P], F32R)
        top, neg, total, inv = (ph.sb(n, [P, MEM_HEADS]) for n in ("top", "neg", "total", "inv"))
        prob = ph.sb("prob", [P, MEM_HEADS, MEM_TOKENS])
        prob_t = ph.sb("prob_t", [P, MEM_HEADS, MT, P])
        m_hi = ph.sb("m_hi", [P, 2, ALLP, P], F32R)
        m_lo = ph.sb("m_lo", [P, 2, ALLP, P], F32R)
        ps_var = ph.ps("ps_var", [P, 512])
        ps_att = ph.ps("ps_att", [P, 512])
        ps_s = ph.ps("ps_s", [P, MEM_HEADS, MEM_TOKENS])
        ps_y = [ph.ps(f"ps_y{i}", [P, 512]) for i in range(4)]

        names = ("consts_in kb_ready kbhi_ready kblo_ready whi_ready wlo_ready squared summed var_ready log_ready root0 dve rooted "
                 "normed qhi_ready qlo_ready scored top_ready exped prob_ready p_turned pt_ready attended gated_mix gated split_hi "
                 "split_lo y_ready added gain_ready").split()
        s = {n: ph.sem(n) for n in names}
        (consts_in, kb_ready, kbhi_ready, kblo_ready, whi_ready, wlo_ready, squared, summed, var_ready, log_ready, root0, dve, rooted,
         normed, qhi_ready, qlo_ready, scored, top_ready, exped, prob_ready, p_turned, pt_ready, attended, gated_mix, gated, split_hi,
         split_lo, y_ready, added, gain_ready) = (s[n] for n in names)
        w_loaded = [ph.sem(f"w_loaded{c}") for c in range(ALLP)]
        loaded = [ph.sem(f"loaded{i}") for i in range(R)]
        x_loaded = [ph.sem(f"x_loaded{i}") for i in range(XR)]
        stored = [ph.sem(f"stored{i}") for i in range(XR)]
        DMAS = 3
        block = ph.block()

        STEPS = range(-3, TILES)
        W_STEPS = ((0, 1, 2), (3, 4, 5), (6, 7))

        def here(t):
            return 0 <= t < TILES

        @block.sync
        def _(sp):
            w_l = w_out[bass.ds(layer, 1)].rearrange("o (c p) n -> (o p) c n", p=P)
            mix_v = mixed.rearrange("(b p) n -> p b n", p=P)
            mem_q = proj[MEMQ * P:GATE0 * P, :].rearrange("(b p) n -> p b n", p=P)
            gates = proj[GATE0 * P:NBLK * P, :].rearrange("(b p) n -> p b n", p=P)

            def load(t):
                at, cols = t % R, slice(t * P, (t + 1) * P)
                if t >= R:
                    sp.wait_ge(split_lo, t - R + 1)
                sp.dma_start(m[:, at, 0:MIXP, :], mix_v[:, :, cols]).then_inc(loaded[at], 16)
                sp.dma_start(m[:, at, MIXP:ALLP, :], mem_q[:, :, cols]).then_inc(loaded[at], 16)
                sp.dma_start(g[:, at, :, :], gates[:, :, cols]).then_inc(loaded[at], 16)

            def load_x(t):
                if t >= XR:
                    sp.wait_ge(stored[t % XR], 16 * (t // XR))
                sp.dma_start(x_t[:, t % XR, :], x_run[t * P:(t + 1) * P, :]).then_inc(x_loaded[t % XR], 16)

            load(0)
            sp.dma_start(k_raw[:, :, :], mem_k[bass.ds(layer, 1)].rearrange("o p (a n) -> (o p) a n", a=MEMP)).then_inc(consts_in, 16)
            sp.dma_start(m_v[:, :, :], mem_v[bass.ds(layer, 1)].rearrange("o p (a n) -> (o p) a n", a=MT)).then_inc(consts_in, 16)
            sp.dma_start(r_g[:, :], ret_norm_g[bass.ds(layer, 1)].rearrange("o (c p) -> (o p) c", p=P),
                         allow_slow_non_contiguous=True).then_inc(consts_in, 16)
            for t in range(1, R):
                for c in W_STEPS[t - 1]:
                    sp.dma_start(wo_raw[:, c, :], w_l[:, c, :]).then_inc(w_loaded[c], 16)
                load(t)
            load_x(0)
            for t in range(TILES + 1):
                if here(t + R):
                    load(t + R)
                if here(t + 1):
                    load_x(t + 1)
                if t:
                    sp.wait_ge(added, 2 * t)
                    sp.dma_start(x_run[(t - 1) * P:t * P, :], x_t[:, (t - 1) % XR, :]).then_inc(stored[(t - 1) % XR], 16)
            for i in range(XR):
                sp.wait_ge(stored[i], 16 * len(range(i, TILES, XR)))

        @block.scalar
        def _(act):
            def square(t):
                act.wait_ge(loaded[t % R], 16 * DMAS * (t // R + 1))
                if t:
                    act.wait_ge(summed, t)
                nc.scalar.activation(sq[:, :, :], m[:, t % R, SBP:ALLP, :], ACT.Square).then_inc(squared, 1)

            def q_split(t):
                if t >= 2:
                    act.wait_ge(scored, t - 1)
                nc.scalar.copy(q_hi[:, t % 2, :, :], m[:, t % R, MIXP:ALLP, :]).then_inc(qhi_ready, 1)

            def roots(t):
                act.wait_ge(var_ready, t + 1)
                nc.scalar.activation(tmp[:, :], var[:, :], ACT.Ln).then_inc(log_ready, 1)
                act.wait_ge(log_ready, t + 1)
                nc.scalar.activation(root[:, t % 2, :], tmp[:, :], ACT.Exp, scale=-0.5).then_inc(root0, 1)

            def exps(t):
                act.wait_ge(top_ready, t + 1)
                if t:
                    act.wait_ge(p_turned, t)
                for h in range(MEM_HEADS):
                    nc.scalar.activation(prob[:, h, :], ps_s[:, h, :], ACT.Exp, bias=neg[:, h:h + 1],
                                         scale=root[:, t % 2, NR + h:NR + h + 1], accum_out=total[:, h:h + 1]).then_inc(exped, 1)

            def turned(t):
                act.wait_ge(p_turned, t + 1)
                if t:
                    act.wait_ge(attended, t)
                nc.scalar.copy(prob_t[:, :, :, :], ps_s[:, :, :].rearrange("p h (b n) -> p h b n", n=P)).then_inc(pt_ready, 1)

            def split(t):
                act.wait_ge(gated, t + 1)
                if t >= 2:
                    act.wait_ge(y_ready, 2 * (t - 1))
                nc.scalar.copy(m_hi[:, t % 2, :, :], m[:, t % R, :, :]).then_inc(split_hi, 1)

            nc.scalar.preload_act_table_set("natural_log_exp_and_others")
            square(0)
            q_split(0)
            act.wait_ge(kb_ready, 3)
            nc.scalar.copy(kb_hi[:, :, :], kb_raw[:, :, :, :].rearrange("p a b n -> p a (b n)")).then_inc(kbhi_ready, 1)
            for t in STEPS:
                if here(t + 2):
                    exps(t + 2)
                if here(t + 3):
                    roots(t + 3)
                if here(t + 1):
                    split(t + 1)
                if here(t + 4):
                    square(t + 4)
                    q_split(t + 4)
                if here(t + 2):
                    turned(t + 2)
                if t < 0:
                    for c in W_STEPS[t + 3]:
                        act.wait_ge(w_loaded[c], 16)
                        nc.scalar.copy(wo_hi[:, c, :], wo_raw[:, c, :]).then_inc(whi_ready, 1)

        @block.vector
        def _(v):
            n_dve = [0]

            def step(ins):
                n_dve[0] += 1
                ins.then_inc(dve, 1)
                v.wait_ge(dve, n_dve[0])

            def variance(t):
                v.wait_ge(summed, t + 1)
                if t:
                    v.wait_ge(rooted, t)
                nc.vector.tensor_scalar(var[:, :], ps_var[:, 0:NVAR], EPS, None, ALU.add).then_inc(var_ready, 1)

            def norm(t):
                v.wait_ge(root0, t + 1)
                v.wait_ge(var_ready, t + 1)
                r = root[:, t % 2, :]
                step(nc.vector.tensor_tensor(tmp[:, :], r, r, ALU.mult))
                step(nc.vector.scalar_tensor_tensor(tmp[:, :], tmp[:, :], -0.5, var[:, :], ALU.mult, ALU.mult))
                nc.vector.scalar_tensor_tensor(r, tmp[:, :], 1.5, r, ALU.add, ALU.mult).then_inc(rooted, 1)
                v.wait_ge(rooted, t + 1)
                nc.vector.tensor_tensor(m[:, t % R, SBP:MIXP, :], m[:, t % R, SBP:MIXP, :],
                                        r[:, 0:NR].rearrange("p (b n) -> p b n", n=P), ALU.mult).then_inc(normed, 1)

            def tops(t):
                v.wait_ge(scored, t + 1)
                step(nc.vector.tensor_reduce(top[:, :], ps_s[:, :, :], AX.X, ALU.max))
                nc.vector.scalar_tensor_tensor(neg[:, :], top[:, :], -1.0, root[:, t % 2, NR:NVAR], ALU.mult, ALU.mult).then_inc(top_ready, 1)

            def probs(t):
                v.wait_ge(exped, MEM_HEADS * (t + 1))
                step(nc.vector.reciprocal(inv[:, :], total[:, :]))
                for h in range(MEM_HEADS):
                    ins = nc.vector.tensor_scalar(prob[:, h, :], prob[:, h, :], inv[:, h:h + 1], None, ALU.mult)
                ins.then_inc(prob_ready, 1)

            def gate_mix(t):
                v.wait_ge(gain_ready, t + 1)
                v.wait_ge(normed, t + 1)
                nc.vector.tensor_tensor(m[:, t % R, 0:MIXP, :], m[:, t % R, 0:MIXP, :], g[:, t % R, 0:MIXP, :], ALU.mult).then_inc(gated_mix, 1)

            def gate_mem(t):
                v.wait_ge(attended, t + 1)
                v.wait_ge(qlo_ready, t + 1)
                v.wait_ge(squared, t + 1)
                nc.vector.tensor_tensor(m[:, t % R, MIXP:ALLP, :], ps_att[:, 0:MEMP * P].rearrange("p (b n) -> p b n", n=P),
                                        g[:, t % R, MIXP:ALLP, :], ALU.mult).then_inc(gated, 1)

            def add(t, half):
                v.wait_ge(y_ready, 2 * t + half + 1)
                if half == 0:
                    v.wait_ge(x_loaded[t % XR], 16 * (t // XR + 1))
                cols = slice(half * 512, (half + 1) * 512)
                nc.vector.tensor_tensor(x_t[:, t % XR, cols], ps_y[2 * (t % 2) + half][:, :], x_t[:, t % XR, cols], ALU.add).then_inc(added, 1)

            nc.vector.memset(kb_raw[:, :, :, :], 0.0).then_inc(kb_ready, 1)
            v.wait_ge(kb_ready, 1)
            v.wait_ge(consts_in, 48)
            for i in range(2):
                rows = slice(i * HD, (i + 1) * HD)
                nc.vector.tensor_copy(kb_raw[rows, :, i, :], k_raw[rows, :, :]).then_inc(kb_ready, 1)
            v.wait_ge(kbhi_ready, 1)
            nc.vector.tensor_tensor(kb_lo[:, :, :], kb_raw[:, :, :, :].rearrange("p a b n -> p a (b n)"), kb_hi[:, :, :],
                                    ALU.subtract).then_inc(kblo_ready, 1)
            for t in STEPS:
                if here(t + 2):
                    tops(t + 2)
                if here(t + 3):
                    variance(t + 3)
                if here(t - 1):
                    add(t - 1, 1)
                if here(t + 2):
                    gate_mix(t + 2)
                    probs(t + 2)
                if here(t + 3):
                    norm(t + 3)
                if here(t):
                    add(t, 0)
                if here(t + 2):
                    gate_mem(t + 2)
                if t < 0:
                    for c in W_STEPS[t + 3]:
                        v.wait_ge(whi_ready, c + 1)
                        nc.vector.tensor_tensor(wo_lo[:, c, :], wo_raw[:, c, :], wo_hi[:, c, :], ALU.subtract).then_inc(wlo_ready, 1)
            add(TILES - 1, 1)

        @block.gpsimd
        def _(pool):
            def gains(t):
                pool.wait_ge(loaded[t % R], 16 * DMAS * (t // R + 1))
                nc.gpsimd.tensor_tensor(g[:, t % R, SBP:MIXP, :], g[:, t % R, SBP:MIXP, :], wide(r_g[:, :], P), ALU.mult).then_inc(gain_ready, 1)

            def q_split(t):
                pool.wait_ge(qhi_ready, t + 1)
                if t >= 2:
                    pool.wait_ge(scored, t - 1)
                nc.gpsimd.tensor_tensor(q_lo[:, t % 2, :, :], m[:, t % R, MIXP:ALLP, :], q_hi[:, t % 2, :, :], ALU.subtract).then_inc(qlo_ready, 1)

            def split(t):
                pool.wait_ge(split_hi, t + 1)
                if t >= 2:
                    pool.wait_ge(y_ready, 2 * (t - 1))
                nc.gpsimd.tensor_tensor(m_lo[:, t % 2, :, :], m[:, t % R, :, :], m_hi[:, t % 2, :, :], ALU.subtract).then_inc(split_lo, 1)

            pool.wait_ge(consts_in, 48)
            gains(0)
            q_split(0)
            for t in STEPS:
                if here(t + 1):
                    split(t + 1)
                if here(t + 4):
                    gains(t + 4)
                    q_split(t + 4)

        @block.tensor
        def _(pe):
            def sums(t):
                pe.wait_ge(squared, t + 1)
                if t:
                    pe.wait_ge(var_ready, t)
                nc.tensor.matmul(ps_var[:, 0:NR], cst[:, C_AVG:C_AVG + P], sq[:, 0:RETP, :].rearrange("p b n -> p (b n)"), start=True, stop=True)
                for p in range(MEMP):
                    mm = nc.tensor.matmul(ps_var[:, NR + 2 * p:NR + 2 * p + 2], sq[:, RETP + p, :], cst[:, C_AVG:C_AVG + P:HD],
                                          start=True, stop=True)
                mm.then_inc(summed, 1)

            def scores(t):
                pe.wait_ge(qhi_ready, t + 1)
                pe.wait_ge(qlo_ready, t + 1)
                if t:
                    pe.wait_ge(pt_ready, t)
                for p in range(MEMP):
                    to = ps_s[:, 2 * p:2 * p + 2, :].rearrange("p h n -> p (h n)")
                    nc.tensor.matmul(to, q_hi[:, t % 2, p, :], kb_hi[:, p, :], start=True, stop=False)
                    nc.tensor.matmul(to, q_hi[:, t % 2, p, :], kb_lo[:, p, :], start=False, stop=False)
                    mm = nc.tensor.matmul(to, q_lo[:, t % 2, p, :], kb_hi[:, p, :], start=False, stop=True)
                mm.then_inc(scored, 1)

            def turn(t):
                pe.wait_ge(prob_ready, t + 1)
                for h in range(MEM_HEADS):
                    for b in range(MT):
                        mm = nc.tensor.transpose(ps_s[:, h, b * P:(b + 1) * P], prob[:, h, b * P:(b + 1) * P], cst[:, C_ID:C_ID + P])
                mm.then_inc(p_turned, 1)

            def attend(t):
                pe.wait_ge(pt_ready, t + 1)
                if t:
                    pe.wait_ge(gated, t)
                for h in range(MEM_HEADS):
                    rows = slice((h % 2) * HD, (h % 2 + 1) * HD)
                    for b in range(MT):
                        mm = nc.tensor.matmul(ps_att[rows, (h // 2) * P:(h // 2 + 1) * P], m_v[:, b, h * HD:(h + 1) * HD],
                                              prob_t[:, h, b, :], start=b == 0, stop=b == MT - 1)
                mm.then_inc(attended, 1)

            def project_part(t, part):
                half, quarter = part // 2, part % 2
                if part == 0:
                    pe.wait_ge(split_hi, t + 1)
                    pe.wait_ge(split_lo, t + 1)
                if quarter == 0 and t >= 2:
                    pe.wait_ge(added, 2 * (t - 2) + half + 1)
                cols = slice(half * 512, (half + 1) * 512)
                for c in range(quarter * ALLP // 2, (quarter + 1) * ALLP // 2):
                    if t == 0 and part < 2:
                        pe.wait_ge(wlo_ready, c + 1)
                    for i, (a, w) in enumerate(((m_hi, wo_hi), (m_hi, wo_lo), (m_lo, wo_hi))):
                        mm = nc.tensor.matmul(ps_y[2 * (t % 2) + half][:, :], a[:, t % 2, c, :], w[:, c, cols],
                                              start=c == 0 and i == 0, stop=c == ALLP - 1 and i == 2)
                if quarter == 1:
                    mm.then_inc(y_ready, 1)

            pe.wait_ge(consts_in, 48)
            pe.wait_ge(kbhi_ready, 1)
            pe.wait_ge(kblo_ready, 1)
            for t in STEPS:
                if here(t + 2):
                    scores(t + 2)
                if here(t + 3):
                    sums(t + 3)
                if here(t):
                    project_part(t, 0)
                    project_part(t, 1)
                if here(t + 2):
                    turn(t + 2)
                if here(t):
                    project_part(t, 2)
                if here(t + 2):
                    attend(t + 2)
                if here(t):
                    project_part(t, 3)



_INS = ["x", "mem", "positions", "norm_g", "w_in", "w_out", "mem_norm_g", "w_mem_kv", "mem_q_norm_g", "mem_k_norm_g", "ret_norm_g"]


def kernel(**inputs):
    import concourse.bacc as bacc
    from concourse.bass_utils import run_bass_kernel_spmd

    nc = bacc.Bacc("TRN2", target_bir_lowering=False, num_devices=1)
    arrays, args = {}, []
    for name in _INS:
        arrays[f"in_{name}"] = np.ascontiguousarray(inputs[name])
    arrays["in_consts"] = constants()
    for name, a in arrays.items():
        args.append(nc.dram_tensor(name, a.shape, mybir.dt.from_np(a.dtype), kind="ExternalInput").ap())
    out = nc.dram_tensor("out_x", (1, SEQ, D_MODEL), F32, kind="ExternalOutput").ap()
    build(nc, *args, out)
    r = run_bass_kernel_spmd(nc, [arrays], core_ids=[0])
    return r.results[0]["out_x"]
```

```python
from contextlib import ExitStack

import numpy as np

import concourse.bass as bass
from concourse import mybir

F32 = mybir.dt.float32
F32R = mybir.dt.float32r
BF16 = mybir.dt.bfloat16
I32 = mybir.dt.int32
ALU = mybir.AluOpType
ACT = mybir.ActivationFunctionType
AX = mybir.AxisListType

P = 128
D_MODEL = 1024
SEQ = 2048
DEPTH = 2
HD = 64
SB_HEADS, RET_HEADS, MEM_HEADS = 6, 6, 4
MEM_TOKENS = 256
IN_WIDTH = (4 * SB_HEADS + 4 * RET_HEADS + 2 * MEM_HEADS) * HD
EPS = 1e-6
ROPE_BASE = 10000.0

KC = D_MODEL // P
TILES = SEQ // P
SPAN = 512
SPANS = SEQ // SPAN
NBLK = IN_WIDTH // P
SBP, RETP, MEMP = SB_HEADS // 2, RET_HEADS // 2, MEM_HEADS // 2

_SB, _RET, _MEM = 0, 4 * SBP, 4 * SBP + 4 * RETP
ORDER = list(range(_SB, _SB + 2 * SBP))
RETQ = len(ORDER)
ORDER += range(_RET, _RET + 2 * RETP)
SBV = len(ORDER)
ORDER += range(_SB + 2 * SBP, _SB + 3 * SBP)
RETV = len(ORDER)
ORDER += range(_RET + 2 * RETP, _RET + 3 * RETP)
MEMQ = len(ORDER)
ORDER += range(_MEM, _MEM + MEMP)
GATE0 = len(ORDER)
ORDER += (list(range(_SB + 3 * SBP, _SB + 4 * SBP)) + list(range(_RET + 3 * RETP, _RET + 4 * RETP))
          + list(range(_MEM + MEMP, _MEM + 2 * MEMP)))
KINDS = (("split", 0, RETQ), ("rotate", RETQ, SBV), ("plain", SBV, GATE0), ("gate", GATE0, NBLK))
MIXP = SBP + RETP
ALLP = MIXP + MEMP

C_ID, C_MASK, C_AVG = 0, P, 2 * P
C_DEC = 3 * P
C_QD = C_DEC + RET_HEADS * P
C_KD = C_QD + RETP * P
C_CD = C_KD + RET_HEADS
C_FREQ = C_CD + RETP
C_SIGN = C_FREQ + 1
C_ALL = C_SIGN + 1


def constants():
    c = np.zeros((P, C_ALL), np.float64)
    i = np.arange(P)
    c[:, C_ID:C_ID + P] = np.eye(P)
    c[:, C_MASK:C_MASK + P] = np.where(i[None, :] >= i[:, None], -1e30, 0.0)
    c[:, C_AVG:C_AVG + P] = (i[:, None] // HD == i[None, :] // HD) / HD
    lg = np.log(1.0 - 2.0 ** (-5.0 - np.arange(RET_HEADS)))
    gap = i[None, :] - i[:, None]
    for h in range(RET_HEADS):
        c[:, C_DEC + h * P:C_DEC + (h + 1) * P] = np.where(gap >= 0, np.exp(lg[h] * np.maximum(gap, 0)), 0) * HD ** -0.5
        c[:, C_KD + h] = np.exp(lg[h] * (P - 1 - i)) * HD ** -0.5
        rows = slice((h % 2) * HD, (h % 2 + 1) * HD)
        c[rows, C_QD + h // 2 * P:C_QD + (h // 2 + 1) * P] = np.exp(lg[h] * (i + 1))[None, :]
        c[rows, C_CD + h // 2] = np.exp(lg[h] * P)
    c[:, C_FREQ] = ROPE_BASE ** (-(i % (HD // 2)) / (HD // 2))
    c[:, C_SIGN] = np.where(i % HD < HD // 2, 1.0, -1.0)
    return c.astype(np.float32)


def wide(ap, n):
    return ap.unsqueeze(2).broadcast_to([ap.shape[0], ap.shape[1], n])


def build(nc, x, mem, positions, norm_g, w_in, w_out, mem_norm_g, w_mem_kv, mem_q_norm_g, mem_k_norm_g,
          ret_norm_g, consts, out):
    proj = nc.dram_tensor("proj", (NBLK * P, SEQ), F32, kind="Internal").ap()
    proj_lo = nc.dram_tensor("proj_lo", (RETQ * P, SEQ), F32, kind="Internal").ap()
    mixed = nc.dram_tensor("mixed", (MIXP * P, SEQ), F32, kind="Internal").ap()
    rotary = nc.dram_tensor("rotary", (2 * P, SEQ), F32, kind="Internal").ap()
    mem_k = nc.dram_tensor("mem_k", (DEPTH, P, MEMP * MEM_TOKENS), F32, kind="Internal").ap()
    mem_v = nc.dram_tensor("mem_v", (DEPTH, P, 2 * MEM_HEADS * HD), F32, kind="Internal").ap()
    x_in = x.rearrange("b s d -> (b s) d")
    x_run = out.rearrange("b s d -> (b s) d")

    with ExitStack() as ctx:
        cst = ctx.enter_context(nc.sbuf_tensor("cst", [P, C_ALL], F32))
        prologue(nc, cst, x_in, x_run, mem, positions, mem_norm_g, w_mem_kv, mem_q_norm_g, mem_k_norm_g,
                 consts, rotary, mem_k, mem_v)
        with nc.Fori(0, DEPTH) as layer:
            project(nc, cst, layer, x_run, norm_g, w_in, rotary, proj, proj_lo)
            mix(nc, cst, proj, proj_lo, mixed)
            emit(nc, cst, layer, proj, mixed, mem_k, mem_v, ret_norm_g, w_out, x_run)


class Phase:

    def __init__(self, nc, name):
        self.nc, self.name, self.sems = nc, name, []

    def __enter__(self):
        self.stack = ExitStack()
        self.inner = ExitStack()
        return self

    def sb(self, name, shape, dt=F32):
        return self.stack.enter_context(self.nc.sbuf_tensor(f"{self.name}_{name}", shape, dt))

    def ps(self, name, shape):
        return self.stack.enter_context(self.nc.psum_tensor(f"{self.name}_{name}", shape, F32))

    def sem(self, name):
        s = self.stack.enter_context(self.nc.semaphore(f"{self.name}_{name}"))
        self.sems.append(s)
        return s

    def block(self):
        return self.inner.enter_context(self.nc.Block())

    def __exit__(self, *e):
        self.inner.__exit__(*e)
        if e[0] is None:
            for s in self.sems:
                self.nc.sync.sem_clear(s)
            self.nc.all_engine_barrier()
        self.stack.__exit__(*e)



def prologue(nc, cst, x_in, x_run, mem, positions, mem_norm_g, w_mem_kv, gq, gk, consts, rotary, mem_k, mem_v):
    MT = MEM_TOKENS // P
    KV = 2 * MEM_HEADS * HD
    KW = MEM_HEADS * HD
    NV = DEPTH * MT * MEM_HEADS
    with Phase(nc, "pro") as ph:
        pos_i = ph.sb("pos_i", [P, SEQ], I32)
        ang = ph.sb("ang", [P, SEQ])
        turns = ph.sb("turns", [P, SEQ])
        rest = ph.sb("rest", [P, SEQ])
        table = ph.sb("table", [P, 2, SEQ])
        m_rows = ph.sb("m_rows", [P, MT, D_MODEL])
        junk = ph.sb("junk", [P, D_MODEL])
        var = ph.sb("var", [P, MT + NV])
        y = ph.sb("y", [P, MT + NV])
        t = ph.sb("t", [P, MT + NV])
        m_cols = ph.sb("m_cols", [P, KC, MEM_TOKENS])
        m_g = ph.sb("m_g", [P, DEPTH, KC])
        mg_cols = ph.sb("mg_cols", [P, DEPTH, KC, MEM_TOKENS])
        w_kv = ph.sb("w_kv", [P, DEPTH, KC, KV])
        qk_g = ph.sb("qk_g", [P, 2, DEPTH])
        g_all = ph.sb("g_all", [P, DEPTH])
        ksq = ph.sb("ksq", [P, DEPTH * MT, KW])
        kn = ph.sb("kn", [P, DEPTH * MT, KW])
        k_out = ph.sb("k_out", [P, DEPTH, MEMP * MEM_TOKENS])
        v_out = ph.sb("v_out", [P, DEPTH, MT, KW])
        ps_t = ph.ps("ps_t", [P, 4, 512])
        ps_kv = ph.ps("ps_kv", [P, DEPTH * MT, 512])

        cst_in, pos_in, mem_in, g_in, qk_in = (ph.sem(n) for n in ("cst_in", "pos_in", "mem_in", "g_in", "qk_in"))
        w_loaded = [ph.sem(f"w_loaded{l}") for l in range(DEPTH)]
        x_copied, stored = ph.sem("x_copied"), ph.sem("stored")
        table_ready, table_stored = ph.sem("table_ready"), ph.sem("table_stored")
        sq_ready, root_ready, turned, kv_ready, k_turned = (
            ph.sem(n) for n in ("sq_ready", "root_ready", "turned", "kv_ready", "k_turned"))
        dve, act = ph.sem("dve"), ph.sem("act")
        var_ready, rows_ready, cols_ready, kn_ready, out_ready, ang_ready = (
            ph.sem(n) for n in ("var_ready", "rows_ready", "cols_ready", "kn_ready", "out_ready", "ang_ready"))
        block = ph.block()

        @block.sync
        def _(sp):
            sp.dma_start(m_rows[:, :, :], mem[0].rearrange("(m p) d -> p m d", p=P)).then_inc(mem_in, 16)
            sp.dma_start(cst[:, :], consts).then_inc(cst_in, 16)
            for l in range(DEPTH):
                sp.dma_start(w_kv[:, l, :, :], w_mem_kv[l].rearrange("(c p) n -> p c n", p=P)).then_inc(w_loaded[l], 16)
                sp.dma_start(m_g[:, l, :], mem_norm_g[l].rearrange("(c p) -> p c", p=P),
                             allow_slow_non_contiguous=True).then_inc(g_in, 16)
            sp.dma_start(pos_i[:, :], positions.broadcast_to([P, SEQ])).then_inc(pos_in, 16)
            for l in range(DEPTH):
                for half in range(2):
                    for i, g in enumerate((gq, gk)):
                        sp.dma_start(qk_g[half * HD:(half + 1) * HD, i, l:l + 1],
                                     g[l].rearrange("(d o) -> d o", o=1)).then_inc(qk_in, 16)
            for i in range(2):
                sp.wait_ge(table_ready, i + 1)
                sp.dma_start(rotary[i * P:(i + 1) * P, :], table[:, i, :]).then_inc(table_stored, 16)
            sp.wait_ge(out_ready, 1)
            sp.dma_start(mem_v.rearrange("l p n -> p l n"), v_out[:, :, :, :].rearrange("p l m n -> p l (m n)")).then_inc(stored, 16)
            sp.wait_ge(out_ready, DEPTH + 1)
            sp.dma_start(mem_k.rearrange("l p n -> p l n"), k_out[:, :, :]).then_inc(stored, 16)
            sp.wait_ge(table_stored, 32)
            sp.wait_ge(stored, 32)
            sp.wait_ge(x_copied, 16 * 4)

        @block.gpsimd
        def _(pool):
            pool.wait_ge(mem_in, 16)
            for i in range(4):
                rows = slice(i * SEQ // 4, (i + 1) * SEQ // 4)
                pool.dma_start(x_run[rows, :], x_in[rows, :]).then_inc(x_copied, 16)

        @block.scalar
        def _(act_e):
            nc.scalar.preload_act_table_set("natural_log_exp_and_others")
            act_e.wait_ge(mem_in, 16)
            for m in range(MT):
                if m:
                    act_e.wait_ge(sq_ready, m)
                nc.scalar.activation(junk[:, :], m_rows[:, m, :], ACT.Square, accum_out=var[:, m:m + 1]).then_inc(sq_ready, 1)
            act_e.wait_ge(var_ready, 1)
            nc.scalar.activation(t[:, 0:MT], var[:, 0:MT], ACT.Ln).then_inc(act, 1)
            act_e.wait_ge(act, 1)
            nc.scalar.activation(y[:, 0:MT], t[:, 0:MT], ACT.Exp, scale=-0.5).then_inc(root_ready, 1)
            act_e.wait_ge(ang_ready, 1)
            nc.scalar.activation(table[:, 0, :], rest[:, :], ACT.Sin).then_inc(table_ready, 1)
            act_e.wait_ge(ang_ready, 2)
            nc.scalar.activation(table[:, 1, :], turns[:, :], ACT.Sin, scale=cst[:, C_SIGN:C_SIGN + 1]).then_inc(table_ready, 1)
            nc.scalar.preload_act_table_set("natural_log_exp_and_others")
            for k in range(DEPTH * MT):
                act_e.wait_ge(kv_ready, k + 1)
                nc.scalar.activation(ksq[:, k, :], ps_kv[:, k, 0:KW], ACT.Square).then_inc(sq_ready, 1)
            act_e.wait_ge(var_ready, 2)
            nc.scalar.activation(t[:, MT:MT + NV], var[:, MT:MT + NV], ACT.Ln).then_inc(act, 1)
            act_e.wait_ge(act, 2)
            nc.scalar.activation(y[:, MT:MT + NV], t[:, MT:MT + NV], ACT.Exp, scale=-0.5).then_inc(root_ready, 1)

        @block.tensor
        def _(pe):
            pe.wait_ge(cst_in, 16)
            pe.wait_ge(rows_ready, MT)
            for c in range(KC):
                for m in range(MT):
                    k = c * MT + m
                    mm = nc.tensor.transpose(ps_t[:, k // 4, (k % 4) * P:(k % 4 + 1) * P], m_rows[:, m, c * P:(c + 1) * P],
                                             cst[:, C_ID:C_ID + P])
            mm.then_inc(turned, 1)
            for l in range(DEPTH):
                pe.wait_ge(cols_ready, l + 2)
                pe.wait_ge(w_loaded[l], 16)
                for m in range(MT):
                    for c in range(KC):
                        mm = nc.tensor.matmul(ps_kv[:, l * MT + m, :], mg_cols[:, l, c, m * P:(m + 1) * P], w_kv[:, l, c, :],
                                              start=c == 0, stop=c == KC - 1)
                    mm.then_inc(kv_ready, 1)
            pe.wait_ge(kn_ready, 1)
            for l in range(DEPTH):
                for p in range(MEMP):
                    for m in range(MT):
                        mm = nc.tensor.transpose(ps_t[:, l, (p * MT + m) * P:(p * MT + m + 1) * P], kn[:, l * MT + m, p * P:(p + 1) * P],
                                                 cst[:, C_ID:C_ID + P])
                mm.then_inc(k_turned, 1)

        @block.vector
        def _(v):
            n = [0]

            def step(ins):
                n[0] += 1
                ins.then_inc(dve, 1)
                v.wait_ge(dve, n[0])

            def newton(a, b):
                step(nc.vector.tensor_tensor(t[:, a:b], y[:, a:b], y[:, a:b], ALU.mult))
                step(nc.vector.scalar_tensor_tensor(t[:, a:b], t[:, a:b], -0.5, var[:, a:b], ALU.mult, ALU.mult))
                step(nc.vector.scalar_tensor_tensor(y[:, a:b], t[:, a:b], 1.5, y[:, a:b], ALU.add, ALU.mult))

            v.wait_ge(sq_ready, MT)
            nc.vector.tensor_scalar(var[:, 0:MT], var[:, 0:MT], 1.0 / D_MODEL, EPS, ALU.mult, ALU.add).then_inc(var_ready, 1)
            v.wait_ge(var_ready, 1)
            v.wait_ge(root_ready, 1)
            newton(0, MT)
            for m in range(MT):
                nc.vector.tensor_scalar(m_rows[:, m, :], m_rows[:, m, :], y[:, m:m + 1], None, ALU.mult).then_inc(rows_ready, 1)
            v.wait_ge(turned, 1)
            for j in range(4):
                ins = nc.vector.tensor_copy(m_cols[:, 2 * j:2 * j + 2, :], ps_t[:, j, :].rearrange("p (a n) -> p a n", a=2))
            ins.then_inc(cols_ready, 1)
            v.wait_ge(cols_ready, 1)
            v.wait_ge(g_in, 16 * DEPTH)
            for l in range(DEPTH):
                nc.vector.tensor_tensor(mg_cols[:, l, :, :], m_cols[:, :, :], wide(m_g[:, l, :], MEM_TOKENS), ALU.mult).then_inc(cols_ready, 1)
            v.wait_ge(cst_in, 16)
            v.wait_ge(pos_in, 16)
            step(nc.vector.tensor_copy(ang[:, :], pos_i[:, :]))
            step(nc.vector.tensor_scalar(ang[:, :], ang[:, :], cst[:, C_FREQ:C_FREQ + 1], None, ALU.mult))
            big = 1.5 * 2.0 ** 23
            c1, c2 = 6.28125, 0.0019340515136718750
            c3 = 2 * np.pi - c1 - c2
            for i, dst in ((0, rest), (1, turns)):
                step(nc.vector.tensor_scalar(turns[:, :], ang[:, :], float(1 / (2 * np.pi)), 0.25 if i == 0 else 0.0, ALU.mult, ALU.add))
                step(nc.vector.tensor_scalar(turns[:, :], turns[:, :], big, None, ALU.add))
                step(nc.vector.tensor_scalar(turns[:, :], turns[:, :], big, None, ALU.subtract))
                if i == 0:
                    step(nc.vector.scalar_tensor_tensor(rest[:, :], turns[:, :], -c1, ang[:, :], ALU.mult, ALU.add))
                    step(nc.vector.scalar_tensor_tensor(rest[:, :], turns[:, :], -c2, rest[:, :], ALU.mult, ALU.add))
                    step(nc.vector.scalar_tensor_tensor(rest[:, :], turns[:, :], -float(c3), rest[:, :], ALU.mult, ALU.add))
                    step(nc.vector.tensor_scalar(rest[:, :], rest[:, :], float(np.pi / 2), 3.1415925, ALU.add, ALU.min))
                    nc.vector.tensor_scalar(rest[:, :], rest[:, :], -3.1415925, None, ALU.max).then_inc(ang_ready, 1)
                else:
                    step(nc.vector.scalar_tensor_tensor(ang[:, :], turns[:, :], -c1, ang[:, :], ALU.mult, ALU.add))
                    step(nc.vector.scalar_tensor_tensor(ang[:, :], turns[:, :], -c2, ang[:, :], ALU.mult, ALU.add))
                    step(nc.vector.scalar_tensor_tensor(ang[:, :], turns[:, :], -float(c3), ang[:, :], ALU.mult, ALU.add))
                    nc.vector.tensor_scalar(turns[:, :], ang[:, :], -3.1415925, 3.1415925, ALU.max, ALU.min).then_inc(ang_ready, 1)
            v.wait_ge(qk_in, 16 * 4 * DEPTH)
            step(nc.vector.scalar_tensor_tensor(g_all[:, :], qk_g[:, 0, :], HD ** -0.5, qk_g[:, 1, :], ALU.mult, ALU.mult))
            a, b = MT, MT + NV
            v.wait_ge(sq_ready, MT + DEPTH * MT)
            step(nc.vector.tensor_reduce(var[:, a:b], ksq[:, :, :].rearrange("p m (h d) -> p (m h) d", d=HD), AX.X, ALU.add))
            nc.vector.tensor_scalar(var[:, a:b], var[:, a:b], 1.0 / HD, EPS, ALU.mult, ALU.add).then_inc(var_ready, 1)
            nc.vector.tensor_copy(v_out[:, :, :, :].rearrange("p l m n -> p (l m) n"), ps_kv[:, :, KW:KV]).then_inc(out_ready, 1)
            v.wait_ge(var_ready, 2)
            v.wait_ge(root_ready, 2)
            newton(a, b)
            for k in range(DEPTH * MT):
                ins = nc.vector.tensor_tensor(
                    kn[:, k, :].rearrange("p (h d) -> p h d", d=HD), ps_kv[:, k, 0:KW].rearrange("p (h d) -> p h d", d=HD),
                    wide(y[:, a + k * MEM_HEADS:a + (k + 1) * MEM_HEADS], HD), ALU.mult)
            ins.then_inc(kn_ready, 1)
            for l in range(DEPTH):
                v.wait_ge(k_turned, l + 1)
                nc.vector.tensor_scalar(k_out[:, l, :], ps_t[:, l, :], g_all[:, l:l + 1], None, ALU.mult).then_inc(out_ready, 1)



def project(nc, cst, layer, x_run, norm_g, w_in, rotary, proj, proj_lo):
    XR = 4
    PAIRS = NBLK // 2
    with Phase(nc, "prj") as ph:
        h_hi = ph.sb("h_hi", [P, KC, SEQ], F32R)
        h_lo = ph.sb("h_lo", [P, KC, SEQ], F32R)
        x_t = ph.sb("x_t", [P, XR, D_MODEL])
        table = x_t[:, :, :].rearrange("p (a b) n -> p a (b n)", a=2)
        junk = ph.sb("junk", [P, D_MODEL])
        hg = ph.sb("hg", [P, 2, KC, P])
        g_c = ph.sb("g_c", [P, KC])
        var, y, t, lv = (ph.sb(n, [P, TILES]) for n in ("var", "y", "t", "lv"))
        w_raw = ph.sb("w_raw", [P, 2, KC, P])
        w_hi = ph.sb("w_hi", [P, 2, KC, P], F32R)
        w_lo = ph.sb("w_lo", [P, 2, KC, P], F32R)
        stage = ph.sb("stage", [P, SPANS, SPAN])
        extra = ph.sb("extra", [P, SPANS, SPAN])
        ps_t = [ph.ps(f"ps_t{i}", [P, KC, P]) for i in range(2)]
        ps_a = [ph.ps(f"ps_a{i}", [P, SPAN]) for i in range(SPANS)]

        x_loaded = [ph.sem(f"x_loaded{i}") for i in range(XR)]
        w_loaded = [ph.sem(f"w_loaded{i}") for i in range(2)]
        g_loaded, table_loaded = ph.sem("g_loaded"), ph.sem("table_loaded")
        stored = [ph.sem(f"stored{c}") for c in range(SPANS)]
        lo_stored = [ph.sem(f"lo_stored{c}") for c in range(SPANS)]
        squared, var_ready, log_ready, root_ready, dve, x_scaled = (
            ph.sem(n) for n in ("squared", "var_ready", "log_ready", "root_ready", "dve", "x_scaled"))
        x_turned, hg_ready, hi_ready, lo_ready = (ph.sem(n) for n in ("x_turned", "hg_ready", "hi_ready", "lo_ready"))
        whi_ready, wlo_ready, acc_ready, evacuated, copied, sig_ready, rotated = (
            ph.sem(n) for n in ("whi_ready", "wlo_ready", "acc_ready", "evacuated", "copied", "sig_ready", "rotated"))
        block = ph.block()
        w_l = w_in[bass.ds(layer, 1)].rearrange("o (c p) n -> (o p) c n", p=P)

        def by_pairs(eng, body):
            for kind, n0, n1 in KINDS:
                lo, hi = n0 // 2, n1 // 2
                if lo == 0:
                    body(0, kind, False)
                    lo = 1
                if hi == PAIRS:
                    hi -= 1
                with eng.Fori(lo, hi) as pair:
                    body(pair, kind, False)
            body(PAIRS - 1, KINDS[-1][0], True)

        def parts(pair):
            if isinstance(pair, int) and pair == 0:
                return [(slot, c, 2 * c + slot, (2 * c + slot) % SPANS) for c in range(SPANS) for slot in range(2)]
            return [(slot, c, (2 * pair + slot) * SPANS + c, c) for slot in range(2) for c in range(SPANS)]

        @block.sync
        def _(sp):
            def load_w(n):
                if n >= 2:
                    sp.wait_ge(whi_ready, n - 1)
                    sp.wait_ge(wlo_ready, n - 1)
                b = ORDER[n]
                sp.dma_start(w_raw[:, n % 2, :, :], w_l[:, :, b * P:(b + 1) * P]).then_inc(w_loaded[n % 2], 16)

            def store(kind, n, c, at):
                if c == 0 and 2 <= n + 1 < NBLK:
                    load_w(n + 1)
                cols = slice(c * SPAN, (c + 1) * SPAN)
                if kind == "rotate":
                    sp.wait_ge(rotated, at - SPANS * RETQ + 1)
                else:
                    sp.wait_ge(evacuated, at + 1)
                sp.dma_start(proj[n * P:(n + 1) * P, cols], stage[:, c, :]).then_inc(stored[c], 16)
                if kind == "split":
                    sp.dma_start(proj_lo[n * P:(n + 1) * P, cols], extra[:, c, :]).then_inc(lo_stored[c], 16)

            sp.dma_start(g_c[:, :], norm_g[bass.ds(layer, 1)].rearrange("o (c p) -> (o p) c", p=P),
                         allow_slow_non_contiguous=True).then_inc(g_loaded, 16)
            for i in range(TILES):
                if i >= XR:
                    sp.wait_ge(x_turned, i - XR + 1)
                sp.dma_start(x_t[:, i % XR, :], x_run[i * P:(i + 1) * P, :]).then_inc(x_loaded[i % XR], 16)
                if i in (0, 3):
                    load_w(i // 3)
            sp.wait_ge(x_turned, TILES)
            for i in range(2):
                sp.dma_start(table[:, i, :], rotary[i * P:(i + 1) * P, :]).then_inc(table_loaded, 16)
            for kind, n0, n1 in KINDS:
                for pair in range(n0 // 2, n1 // 2):
                    for slot, c, at, _ in parts(pair):
                        store(kind, 2 * pair + slot, c, at)
            for c in range(SPANS):
                sp.wait_ge(stored[c], 16 * NBLK)
                sp.wait_ge(lo_stored[c], 16 * RETQ)

        @block.scalar
        def _(act):
            def w_split(pair, slot):
                act.wait_ge(w_loaded[slot], (pair + 1) * 16)
                if isinstance(pair, int) and pair == 1 and slot == 0:
                    act.wait_ge(acc_ready, 2 * SPANS - 1)
                elif not (isinstance(pair, int) and pair == 0):
                    act.wait_ge(acc_ready, (2 * pair + slot - 1) * SPANS)
                nc.scalar.copy(w_hi[:, slot, :, :], w_raw[:, slot, :, :]).then_inc(whi_ready, 1)

            def stage_free(n, c):
                if not (isinstance(n, int) and n == 0):
                    act.wait_ge(stored[c], n * 16)

            def evacuate(kind, n, c, at, a):
                if kind == "split":
                    act.wait_ge(acc_ready, at + 1)
                    stage_free(n, c)
                    nc.scalar.copy(stage[:, c, :].bitcast(F32R), a[:, :]).then_inc(copied, 1)
                if kind == "gate":
                    act.wait_ge(acc_ready, at + 1)
                    stage_free(n, c)
                    nc.scalar.activation(stage[:, c, :], a[:, :], ACT.Sigmoid).then_inc(sig_ready, 1)

            def blocks(pair, kind, last):
                first = isinstance(pair, int) and pair == 0
                for slot, c, at, bank in parts(pair):
                    evacuate(kind, 2 * pair + slot, c, at, ps_a[bank])
                    if c == 0 and not first and not (last and slot == 1):
                        w_split(pair + slot, 1 - slot)
                    if first and c == SPANS - 1 and slot == 0:
                        w_split(1, 0)

            nc.scalar.preload_act_table_set("natural_log_exp_and_others")
            for i in range(TILES + 3):
                if i < TILES:
                    act.wait_ge(x_loaded[i % XR], 16 * (i // XR + 1))
                    if i:
                        act.wait_ge(squared, i)
                    nc.scalar.activation(junk[:, :], x_t[:, i % XR, :], ACT.Square, accum_out=var[:, i:i + 1]).then_inc(squared, 1)
                if 0 <= i - 1 < TILES:
                    j = i - 1
                    act.wait_ge(var_ready, j + 1)
                    nc.scalar.activation(lv[:, j:j + 1], var[:, j:j + 1], ACT.Ln).then_inc(log_ready, 1)
                    act.wait_ge(log_ready, j + 1)
                    nc.scalar.activation(y[:, j:j + 1], lv[:, j:j + 1], ACT.Exp, scale=-0.5).then_inc(root_ready, 1)
                if 0 <= i - 3 < TILES:
                    j = i - 3
                    act.wait_ge(hg_ready, j + 1)
                    nc.scalar.copy(h_hi[:, :, j * P:(j + 1) * P], hg[:, j % 2, :, :]).then_inc(hi_ready, 1)
                if i in (1, 2):
                    w_split(0, i - 1)
            by_pairs(act, blocks)

        @block.gpsimd
        def _(pool):
            def w_split(pair, slot):
                n = 2 * pair + slot
                pool.wait_ge(whi_ready, n + 1)
                if isinstance(pair, int) and pair == 1 and slot == 0:
                    pool.wait_ge(acc_ready, 2 * SPANS - 1)
                elif not (isinstance(pair, int) and pair == 0):
                    pool.wait_ge(acc_ready, (n - 1) * SPANS)
                nc.gpsimd.tensor_tensor(w_lo[:, slot, :, :], w_raw[:, slot, :, :], w_hi[:, slot, :, :], ALU.subtract).then_inc(wlo_ready, 1)

            def blocks(pair, kind, last):
                for slot in range(2):
                    n = 2 * pair + slot
                    if not (last and slot == 1) and not (isinstance(pair, int) and pair + slot == 0):
                        w_split(pair + slot, 1 - slot)
                    if kind == "rotate":
                        for c in range(SPANS):
                            pool.wait_ge(evacuated, n * SPANS + c + 1)
                            nc.gpsimd.tensor_tensor(stage[:, c, :], stage[:, c, :], extra[:, c, :], ALU.add).then_inc(rotated, 1)

            for j in range(TILES):
                pool.wait_ge(hi_ready, j + 1)
                nc.gpsimd.tensor_tensor(h_lo[:, :, j * P:(j + 1) * P], hg[:, j % 2, :, :], h_hi[:, :, j * P:(j + 1) * P],
                                        ALU.subtract).then_inc(lo_ready, 1)
                if j in (0, 1):
                    w_split(0, j)
            by_pairs(pool, blocks)

        @block.vector
        def _(v):
            n_dve = [0]

            def step(ins):
                n_dve[0] += 1
                ins.then_inc(dve, 1)
                v.wait_ge(dve, n_dve[0])

            def evacuate(kind, n, c, at, a):
                to, other = stage[:, c, :], extra[:, c, :]
                if kind == "split":
                    v.wait_ge(copied, at + 1)
                    if not (isinstance(n, int) and n == 0):
                        v.wait_ge(lo_stored[c], n * 16)
                    nc.vector.tensor_tensor(other.bitcast(F32R), a[:, :], to.bitcast(F32R), ALU.subtract).then_inc(evacuated, 1)
                elif kind == "rotate":
                    cols = slice(c * SPAN, (c + 1) * SPAN)
                    v.wait_ge(acc_ready, at + 1)
                    v.wait_ge(table_loaded, 32)
                    v.wait_ge(stored[c], n * 16)
                    v.wait_ge(lo_stored[c], 16 * RETQ)
                    nc.vector.tensor_tensor(to, a[:, :], table[:, 0, cols], ALU.mult)
                    for q in range(4):
                        src, dst = slice((q ^ 1) * 32, (q ^ 1) * 32 + 32), slice(q * 32, q * 32 + 32)
                        ins = nc.vector.tensor_tensor(extra[dst, c, :], a[src, :], table[src, 1, cols], ALU.mult)
                    ins.then_inc(evacuated, 1)
                elif kind == "plain":
                    v.wait_ge(acc_ready, at + 1)
                    v.wait_ge(stored[c], n * 16)
                    nc.vector.tensor_copy(to, a[:, :]).then_inc(evacuated, 1)
                else:
                    v.wait_ge(sig_ready, (n - GATE0) * SPANS + c + 1)
                    nc.vector.tensor_tensor(to, a[:, :], to, ALU.mult).then_inc(evacuated, 1)

            def blocks(pair, kind, last):
                for slot, c, at, bank in parts(pair):
                    evacuate(kind, 2 * pair + slot, c, at, ps_a[bank])

            v.wait_ge(g_loaded, 16)
            for i in range(TILES + 2):
                if i < TILES:
                    v.wait_ge(squared, i + 1)
                    nc.vector.tensor_scalar(var[:, i:i + 1], var[:, i:i + 1], 1.0 / D_MODEL, EPS, ALU.mult, ALU.add).then_inc(var_ready, 1)
                if 0 <= i - 1 < TILES:
                    j = i - 1
                    v.wait_ge(root_ready, j + 1)
                    v.wait_ge(var_ready, j + 1)
                    s = slice(j, j + 1)
                    step(nc.vector.tensor_tensor(t[:, s], y[:, s], y[:, s], ALU.mult))
                    step(nc.vector.scalar_tensor_tensor(t[:, s], t[:, s], -0.5, var[:, s], ALU.mult, ALU.mult))
                    step(nc.vector.scalar_tensor_tensor(y[:, s], t[:, s], 1.5, y[:, s], ALU.add, ALU.mult))
                    nc.vector.tensor_scalar(x_t[:, j % XR, :], x_t[:, j % XR, :], y[:, s], None, ALU.mult).then_inc(x_scaled, 1)
                if 0 <= i - 2 < TILES:
                    j = i - 2
                    v.wait_ge(x_turned, j + 1)
                    if j >= 2:
                        v.wait_ge(lo_ready, j - 1)
                    nc.vector.tensor_tensor(hg[:, j % 2, :, :], ps_t[j % 2][:, :, :], wide(g_c[:, :], P), ALU.mult).then_inc(hg_ready, 1)
            by_pairs(v, blocks)

        @block.tensor
        def _(pe):
            def turn(j):
                pe.wait_ge(x_scaled, j + 1)
                if j >= 2:
                    pe.wait_ge(hg_ready, j - 1)
                for k in range(KC):
                    mm = nc.tensor.transpose(ps_t[j % 2][:, k, :], x_t[:, j % XR, k * P:(k + 1) * P], cst[:, C_ID:C_ID + P])
                mm.then_inc(x_turned, 1)

            def matmuls(slot, c, a):
                for k in range(KC):
                    for i, (w, h) in enumerate(((w_hi, h_hi), (w_hi, h_lo), (w_lo, h_hi))):
                        mm = nc.tensor.matmul(a[:, :], w[:, slot, k, :], h[:, k, c * SPAN:(c + 1) * SPAN],
                                              start=k == 0 and i == 0, stop=k == KC - 1 and i == 2)
                mm.then_inc(acc_ready, 1)

            TURNS = ((6, 7), (8, 9), (10, 11), (12, 13, 14, 15), (), (), (), ())
            for j in range(6):
                turn(j)
            pe.wait_ge(whi_ready, 2)
            pe.wait_ge(wlo_ready, 2)
            for slot, c, at, bank in parts(0):
                if slot == 0:
                    pe.wait_ge(hi_ready, 4 * c + 4)
                    pe.wait_ge(lo_ready, 4 * c + 4)
                if at >= SPANS:
                    pe.wait_ge(evacuated, at - SPANS + 1)
                matmuls(slot, c, ps_a[bank])
                for j in TURNS[at]:
                    turn(j)
            with pe.Fori(1, PAIRS) as pair:
                for slot in range(2):
                    pe.wait_ge(whi_ready, 2 * pair + slot + 1)
                    pe.wait_ge(wlo_ready, 2 * pair + slot + 1)
                    for c in range(SPANS):
                        pe.wait_ge(evacuated, (2 * pair + slot - 1) * SPANS + c + 1)
                        matmuls(slot, c, ps_a[c])



class Unit:

    def __init__(self, n, t, h, lo, width, first, last):
        self.n, self.t, self.h, self.lo, self.width, self.first, self.last = n, t, h, lo, width, first, last
        self.row = t * SB_HEADS + h


def units():
    found = []
    for t in range(TILES):
        count = -(-(t + 1) * P // SPAN)
        cuts = [(t + 1) * u // count * P for u in range(count + 1)]
        for h in range(SB_HEADS):
            for u in range(count - 1, -1, -1):
                found.append(Unit(len(found), t, h, cuts[u], cuts[u + 1] - cuts[u], u == count - 1, u == 0))
    return found


def mix(nc, cst, proj, proj_lo, mixed):
    U = units()
    first = [next(u.n for u in U if u.t == t) for t in range(TILES)] + [len(U)]
    SIDE = ("", "turn_v", "", "", "turn_k", "turn_rv", "", "", "", "scores1", "scores2", "", "", "", "out0", "", "out1", "",
            "out2", "", "kv", "", "", "")
    side = {}
    for t in range(TILES):
        n = first[t + 1] - first[t]
        for k, what in enumerate(SIDE):
            if what:
                side.setdefault(first[t] + k * n // len(SIDE), []).append((what, t + 1 if what == "turn_v" else t))
    B, W3 = 4, 3
    SIG, SCAN, WEIGH, TURN, SPLIT, PV, FOLD = range(1, 8)
    STEPS = len(U) + FOLD

    def at(n, stage):
        return (n - stage,) if 0 <= n - stage < len(U) else ()

    with Phase(nc, "mix") as ph:
        k_st = ph.sb("k_st", [P, SB_HEADS, SEQ], F32R)
        v_st = ph.sb("v_st", [P, TILES, SB_HEADS, 2, HD], F32R)
        v_in = ph.sb("v_in", [P, 2, SBP, P])
        r_in = ph.sb("r_in", [P, 2, 3 * RETP, P])
        q_hi = ph.sb("q_hi", [P, 2, SB_HEADS, P], F32R)
        q_lo = ph.sb("q_lo", [P, 2, SB_HEADS, P], F32R)
        eye = ph.sb("eye", [P, P], BF16)
        mask = ph.sb("mask", [P, P], BF16)
        beta = ph.sb("beta", [P, B, SPAN])
        keep = ph.sb("keep", [P, B, SPAN])
        stick = ph.sb("stick", [P, B, SPAN + 1])
        zero = ph.sb("zero", [P, SPAN])
        w_t = ph.sb("w_t", [P, W3, SPAN])
        wt = ph.sb("wt", [P, W3, SPAN // P, 2, P], F32R)
        f1 = ph.sb("f1", [HD, 2, 2 * P])
        f2 = ph.sb("f2", [P, 2, 2 * P])
        o_t = ph.sb("o_t", [P, 2, MIXP, P])
        q_bd = ph.sb("q_bd", [P, 2, RETP, 2 * P])
        q_dec = ph.sb("q_dec", [P, RETP, P])
        k_hat = ph.sb("k_hat", [P, RETP * P])
        r_v = ph.sb("r_v", [P, RETP * P])
        sc = ph.sb("sc", [P, RET_HEADS, P])
        state = ph.sb("state", [P, RETP, P])
        ps_z = [ph.ps(f"ps_z{i}", [P, SPAN]) for i in range(2)]
        ps_w = [ph.ps(f"ps_w{i}", [P, SPAN]) for i in range(2)]
        ps_o = [ph.ps(f"ps_o{i}", [P, 512]) for i in range(2)]
        ps_1 = ph.ps("ps_1", [P, 512])
        ps_2 = ph.ps("ps_2", [P, 512])

        names = ("consts_ready z_ready sig_ready scanned seeded weighted w_turned wt_hi wt_lo pv_ready folded1 folded2 "
                 "folded zeroed qdec_ready "
                 "v_turned v_hi v_lo k_turned rv_turned khat_ready rv_ready scores1_ready scores2_ready sc_ready out_ready "
                 "ret_copied kv_ready "
                 "state_decayed state_ready").split()
        s = {n: ph.sem(n) for n in names}
        (consts_ready, z_ready, sig_ready, scanned, seeded, weighted, w_turned, wt_hi, wt_lo, pv_ready, folded1, folded2,
         folded, zeroed, qdec_ready,
         v_turned, v_hi, v_lo, k_turned, rv_turned, khat_ready, rv_ready, scores1_ready, scores2_ready, sc_ready, out_ready,
         ret_copied, kv_ready,
         state_decayed, state_ready) = (s[n] for n in names)
        k_loaded = [ph.sem(f"k_loaded{i}") for i in range(2)]
        q_loaded = [ph.sem(f"q_loaded{i}") for i in range(2)]
        ret_loaded = [ph.sem(f"ret_loaded{i}") for i in range(2)]
        o_stored = [ph.sem(f"o_stored{i}") for i in range(2)]
        v_loaded = [ph.sem(f"v_loaded{i}") for i in range(2)]
        K_DMAS, Q_DMAS, RET_DMAS = 2, 4, 4
        block = ph.block()

        @block.sync
        def _(sp):
            his = proj[0:RETQ * P, :].rearrange("(h d) n -> d h n", d=HD)
            los = proj_lo.rearrange("(h d) n -> d h n", d=HD)
            values = proj[SBV * P:RETV * P, :].rearrange("(b p) n -> p b n", p=P)
            ret_qk = proj[RETQ * P:SBV * P, :].rearrange("(b p) n -> p b n", p=P)
            ret_q = proj[RETQ * P:(RETQ + RETP) * P, :].rearrange("(b i d) n -> i d b n", i=2, d=HD)
            ret_v = proj[RETV * P:MEMQ * P, :].rearrange("(b p) n -> p b n", p=P)
            to = mixed.rearrange("(b p) n -> p b n", p=P)

            def load_v(t):
                if t >= 2:
                    sp.wait_ge(v_turned, t - 1)
                sp.dma_start(v_in[:, t % 2, :, :], values[:, :, t * P:(t + 1) * P]).then_inc(v_loaded[t % 2], 16)

            def load_k(t):
                at, cols = t % 2, slice(t * P, (t + 1) * P)
                for half, of in enumerate((his, los)):
                    rows = slice(half * HD, (half + 1) * HD)
                    sp.dma_start(k_st[rows, :, cols].bitcast(F32), of[:, SB_HEADS:2 * SB_HEADS, cols]).then_inc(k_loaded[at], 16)

            def load_q(t):
                at, cols = t % 2, slice(t * P, (t + 1) * P)
                if t >= 2:
                    sp.wait_ge(z_ready, first[t - 1])
                for q, of in ((q_hi, his), (q_lo, los)):
                    for half in range(2):
                        rows = slice(half * HD, (half + 1) * HD)
                        sp.dma_start(q[rows, at, :, :].bitcast(F32), of[:, 0:SB_HEADS, cols]).then_inc(q_loaded[at], 16)

            def load_ret(t):
                at, cols = t % 2, slice(t * P, (t + 1) * P)
                if t >= 2:
                    sp.wait_ge(scores2_ready, t - 1)
                    sp.wait_ge(qdec_ready, t - 1)
                elif t == 0:
                    sp.wait_ge(zeroed, 1)
                for i in range(2):
                    rows, at_cols = slice(i * HD, (i + 1) * HD), slice(i * P, (i + 1) * P)
                    sp.dma_start(q_bd[rows, at, :, at_cols], ret_q[i, :, :, cols]).then_inc(ret_loaded[at], 16)
                sp.dma_start(r_in[:, at, 0:2 * RETP, :], ret_qk[:, :, cols]).then_inc(ret_loaded[at], 16)
                sp.dma_start(r_in[:, at, 2 * RETP:3 * RETP, :], ret_v[:, :, cols]).then_inc(ret_loaded[at], 16)

            def store(t):
                sp.wait_ge(folded, SBP * (t + 1))
                sp.wait_ge(ret_copied, t + 1)
                sp.dma_start(to[:, :, t * P:(t + 1) * P], o_t[:, t % 2, :, :]).then_inc(o_stored[t % 2], 16)

            for t in range(2):
                load_v(t)
                load_k(t)
                load_q(t)
                load_ret(t)
            for t in range(TILES + 1):
                if t + 2 < TILES:
                    load_v(t + 2)
                    load_ret(t + 2)
                    load_k(t + 2)
                if t:
                    store(t - 1)
                if t + 2 < TILES:
                    load_q(t + 2)
            for i in range(2):
                sp.wait_ge(o_stored[i], 16 * TILES // 2)

        @block.tensor
        def _(pe):
            def turn_v(t):
                if t >= TILES:
                    return
                pe.wait_ge(v_loaded[t % 2], 16 * (t // 2 + 1))
                if t == 1:
                    pe.wait_ge(v_lo, 1)
                if t >= 2:
                    pe.wait_ge(ret_copied, t - 1)
                for p in range(SBP):
                    mm = nc.tensor.transpose(ps_1[:, p * P:(p + 1) * P], v_in[:, t % 2, p, :], cst[:, C_ID:C_ID + P])
                mm.then_inc(v_turned, 1)

            def turn_k(t):
                pe.wait_ge(ret_loaded[t % 2], 16 * RET_DMAS * (t // 2 + 1))
                pe.wait_ge(v_lo, min(t + 2, TILES))
                pe.wait_ge(v_hi, min(t + 2, TILES))
                if t == TILES - 1:
                    pe.wait_ge(ret_copied, t)
                for p in range(RETP):
                    mm = nc.tensor.transpose(ps_1[:, p * P:(p + 1) * P], r_in[:, t % 2, RETP + p, :], cst[:, C_ID:C_ID + P])
                mm.then_inc(k_turned, 1)

            def turn_rv(t):
                if t >= 1:
                    pe.wait_ge(state_ready, t)
                for p in range(RETP):
                    mm = nc.tensor.transpose(ps_2[:, p * P:(p + 1) * P], r_in[:, t % 2, 2 * RETP + p, :], cst[:, C_ID:C_ID + P])
                mm.then_inc(rv_turned, 1)

            def scores1(t):
                pe.wait_ge(khat_ready, t + 1)
                for p in range(2):
                    mm = nc.tensor.matmul(ps_1[:, p * 2 * P:(p + 1) * 2 * P], r_in[:, t % 2, RETP + p, :], q_bd[:, t % 2, p, :],
                                          start=True, stop=True)
                mm.then_inc(scores1_ready, 1)

            def scores2(t):
                pe.wait_ge(rv_ready, t + 1)
                nc.tensor.matmul(ps_2[:, 0:2 * P], r_in[:, t % 2, RETP + 2, :], q_bd[:, t % 2, 2, :],
                                 start=True, stop=True).then_inc(scores2_ready, 1)

            def ret_out(p):
                def out(t):
                    pe.wait_ge(sc_ready, 2 * t + 2)
                    pe.wait_ge(qdec_ready, t + 1)
                    cols = slice(p * P, (p + 1) * P)
                    if t:
                        nc.tensor.matmul(ps_1[:, cols], state[:, p, :], q_dec[:, p, :], start=True, stop=False, skip_group_check=True)
                    for i in range(2):
                        rows = slice(i * HD, (i + 1) * HD)
                        mm = nc.tensor.matmul(ps_1[rows, cols], r_v[:, p * P + i * HD:p * P + (i + 1) * HD], sc[:, 2 * p + i, :],
                                              start=not t, stop=True, skip_group_check=True)
                    if p == RETP - 1:
                        mm.then_inc(out_ready, 1)
                return out

            def kv(t):
                for p in range(RETP):
                    cols = slice(p * P, (p + 1) * P)
                    mm = nc.tensor.matmul(ps_2[:, cols], k_hat[:, cols], r_v[:, cols], start=True, stop=True)
                mm.then_inc(kv_ready, 1)

            jobs = {"turn_v": turn_v, "turn_k": turn_k, "turn_rv": turn_rv, "scores1": scores1, "scores2": scores2,
                    "out0": ret_out(0), "out1": ret_out(1), "out2": ret_out(2), "kv": kv}
            pe.wait_ge(consts_ready, 4)
            turn_v(0)
            for n in range(STEPS):
                for m in at(n, TURN):
                    pe.wait_ge(weighted, m + 1)
                    if m >= 2:
                        pe.wait_ge(wt_lo, m - 1)
                    for b in range(U[m].width // P):
                        mm = nc.tensor.transpose(ps_w[m % 2][:, b * P:(b + 1) * P], w_t[:, m % W3, b * P:(b + 1) * P], cst[:, C_ID:C_ID + P])
                    mm.then_inc(w_turned, 1)
                for m in at(n, 0):
                    u = U[m]
                    if m == first[u.t]:
                        pe.wait_ge(k_loaded[u.t % 2], 16 * K_DMAS * (u.t // 2 + 1))
                        pe.wait_ge(q_loaded[u.t % 2], 16 * Q_DMAS * (u.t // 2 + 1))
                    if m >= 2:
                        pe.wait_ge(sig_ready, m - 1)
                    z, keys = ps_z[m % 2][:, 0:u.width], k_st[:, u.h, u.lo:u.lo + u.width]
                    nc.tensor.matmul(z, q_hi[:, u.t % 2, u.h, :], keys, start=True, stop=False)
                    mm = nc.tensor.matmul(z, q_lo[:, u.t % 2, u.h, :], keys, start=False, stop=not u.first)
                    if u.first:
                        mm = nc.tensor.matmul(ps_z[m % 2][:, u.width - P:u.width], eye[:, :], mask[:, :], start=False, stop=True)
                    mm.then_inc(z_ready, 1)
                for m in at(n, PV):
                    u = U[m]
                    pe.wait_ge(wt_lo, m + 1)
                    if u.first and u.h == 0:
                        pe.wait_ge(v_hi, u.t + 1)
                        pe.wait_ge(v_lo, u.t + 1)
                    if u.first and u.row >= 2:
                        pe.wait_ge(folded2, u.row - 1)
                    for b in range(u.width // P):
                        mm = nc.tensor.matmul(ps_o[u.row % 2][:, 0:2 * P],
                                              v_st[:, u.lo // P + b, u.h, :, :].rearrange("p a d -> p (a d)"),
                                              wt[:, m % W3, b, :, :].rearrange("p a q -> p (a q)"),
                                              start=u.first and b == 0, stop=u.last and b == u.width // P - 1)
                    mm.then_inc(pv_ready, 1)
                for what, t in side.get(n, ()):
                    jobs[what](t)

        @block.scalar
        def _(act):
            def turn_v(t):
                if t >= TILES:
                    return
                act.wait_ge(v_turned, t + 1)
                nc.scalar.copy(v_st[:, t, :, 0, :], ps_1[:, 0:SBP * P].rearrange("p (h d) -> p h d", d=HD)).then_inc(v_hi, 1)

            def copy_rv(t):
                act.wait_ge(rv_turned, t + 1)
                if t:
                    act.wait_ge(kv_ready, t)
                nc.scalar.copy(r_v[:, :], ps_2[:, 0:RETP * P]).then_inc(rv_ready, 1)

            def ret_out(t):
                act.wait_ge(out_ready, t + 1)
                if t >= 2:
                    act.wait_ge(o_stored[t % 2], 16 * (t // 2))
                nc.scalar.copy(o_t[:, t % 2, SBP:MIXP, :], ps_1[:, 0:RETP * P].rearrange("p (b n) -> p b n", n=P)).then_inc(ret_copied, 1)

            jobs = {"turn_v": turn_v, "turn_rv": copy_rv, "out2": ret_out}
            turn_v(0)
            for n in range(STEPS + 1):
                for m in at(n, SPLIT):
                    act.wait_ge(w_turned, m + 1)
                    if m >= W3:
                        act.wait_ge(pv_ready, m - W3 + 1)
                    blocks = U[m].width // P
                    nc.scalar.copy(wt[:, m % W3, 0:blocks, 0, :], ps_w[m % 2][:, 0:U[m].width].rearrange("p (b n) -> p b n", n=P)).then_inc(wt_hi, 1)
                for m in at(n, FOLD):
                    if U[m].last:
                        r = U[m].row
                        act.wait_ge(pv_ready, m + 1)
                        if r >= 2:
                            act.wait_ge(folded2, r - 1)
                        nc.scalar.copy(f1[:, r % 2, :], ps_o[r % 2][HD:P, 0:2 * P]).then_inc(folded1, 1)
                for m in at(n, SIG):
                    act.wait_ge(z_ready, m + 1)
                    if m >= B:
                        act.wait_ge(weighted, m - B + 1)
                        act.wait_ge(scanned, m - B + 1)
                    z = ps_z[m % 2][:, 0:U[m].width]
                    nc.scalar.activation(keep[:, m % B, 0:U[m].width], z, ACT.Sigmoid, scale=-HD ** -0.5)
                    nc.scalar.activation(beta[:, m % B, 0:U[m].width], z, ACT.Sigmoid, scale=HD ** -0.5).then_inc(sig_ready, 1)
                for what, t in side.get(n - 1, ()):
                    if what in jobs:
                        jobs[what](t)

        @block.vector
        def _(v):
            def turn_v(t):
                if t >= TILES:
                    return
                v.wait_ge(v_hi, t + 1)
                nc.vector.tensor_tensor(v_st[:, t, :, 1, :], ps_1[:, 0:SBP * P].rearrange("p (h d) -> p h d", d=HD),
                                        v_st[:, t, :, 0, :], ALU.subtract).then_inc(v_lo, 1)

            def decay_k(t):
                v.wait_ge(k_turned, t + 1)
                if t:
                    v.wait_ge(kv_ready, t)
                nc.vector.tensor_tensor(k_hat[:, :].rearrange("p (h d) -> p h d", d=HD),
                                        ps_1[:, 0:RETP * P].rearrange("p (h d) -> p h d", d=HD),
                                        wide(cst[:, C_KD:C_KD + RET_HEADS], HD), ALU.mult).then_inc(khat_ready, 1)

            dec = cst[:, C_DEC:C_QD].rearrange("p (h n) -> p h n", n=P)

            def decay_scores1(t):
                v.wait_ge(scores1_ready, t + 1)
                if t:
                    v.wait_ge(out_ready, t)
                nc.vector.tensor_tensor(sc[:, 0:4, :], ps_1[:, :].rearrange("p (h n) -> p h n", n=P), dec[:, 0:4, :],
                                        ALU.mult).then_inc(sc_ready, 1)

            def decay_scores2(t):
                v.wait_ge(scores2_ready, t + 1)
                nc.vector.tensor_tensor(sc[:, 4:6, :], ps_2[:, 0:2 * P].rearrange("p (h n) -> p h n", n=P), dec[:, 4:6, :],
                                        ALU.mult).then_inc(sc_ready, 1)

            def add_state(t):
                v.wait_ge(kv_ready, t + 1)
                v.wait_ge(state_decayed, t + 1)
                for i in range(2):
                    rows, cols = slice(i * HD, (i + 1) * HD), slice(i * HD, (i + 1) * HD)
                    ins = nc.vector.tensor_tensor(state[rows, :, cols], ps_2[rows, 0:RETP * P].rearrange("p (b n) -> p b n", n=P)[:, :, cols],
                                                  state[rows, :, cols], ALU.add)
                ins.then_inc(state_ready, 1)

            jobs = {"turn_v": turn_v, "turn_k": decay_k, "scores1": decay_scores1, "scores2": decay_scores2, "kv": add_state}
            nc.vector.memset(zero[:, :], 0.0).then_inc(consts_ready, 1)
            nc.vector.tensor_copy(eye[:, :], cst[:, C_ID:C_ID + P]).then_inc(consts_ready, 1)
            nc.vector.tensor_copy(mask[:, :], cst[:, C_MASK:C_MASK + P]).then_inc(consts_ready, 1)
            nc.vector.memset(state[:, :, :], 0.0).then_inc(consts_ready, 1)
            v.wait_ge(consts_ready, 4)
            turn_v(0)
            for n in range(STEPS + 1):
                for m in at(n, SCAN):
                    u = U[m]
                    slot, w = m % B, u.width
                    if m >= B:
                        v.wait_ge(weighted, m - B + 1)
                    end = stick[:, slot, w:w + 1]
                    if u.first:
                        nc.vector.memset(end, 1.0).then_inc(seeded, 1)
                        start = 1.0
                    else:
                        v.wait_ge(scanned, m)
                        start = stick[:, (m - 1) % B, 0:1]
                        nc.vector.tensor_copy(end, start).then_inc(seeded, 1)
                    v.wait_ge(sig_ready, m + 1)
                    nc.vector.tensor_tensor_scan(stick[:, slot, 0:w][:, ::-1], keep[:, slot, 0:w][:, ::-1], zero[:, 0:w], start,
                                                 ALU.mult, ALU.add).then_inc(scanned, 1)
                for m in at(n, SPLIT):
                    w = U[m].width
                    v.wait_ge(wt_hi, m + 1)
                    if m >= W3:
                        v.wait_ge(pv_ready, m - W3 + 1)
                    nc.vector.tensor_tensor(wt[:, m % W3, 0:w // P, 1, :], ps_w[m % 2][:, 0:w].rearrange("p (b n) -> p b n", n=P),
                                            wt[:, m % W3, 0:w // P, 0, :], ALU.subtract).then_inc(wt_lo, 1)
                for what, t in side.get(n - 1, ()):
                    if what in jobs:
                        jobs[what](t)
                for m in at(n, FOLD):
                    if U[m].last:
                        u = U[m]
                        r, pair = u.row, u.row // 2
                        v.wait_ge(folded1, r + 1)
                        if pair >= 2:
                            v.wait_ge(folded, pair - 1)
                        rows = slice((u.h % 2) * HD, (u.h % 2 + 1) * HD)
                        nc.vector.tensor_tensor(f2[rows, pair % 2, :], ps_o[r % 2][0:HD, 0:2 * P], f1[:, r % 2, :], ALU.add).then_inc(folded2, 1)

        @block.gpsimd
        def _(pool):
            def decay_q(t):
                pool.wait_ge(ret_loaded[t % 2], 16 * RET_DMAS * (t // 2 + 1))
                if t:
                    pool.wait_ge(out_ready, t)
                nc.gpsimd.tensor_tensor(q_dec[:, :, :], r_in[:, t % 2, 0:RETP, :], cst[:, C_QD:C_KD].rearrange("p (b n) -> p b n", n=P),
                                        ALU.mult).then_inc(qdec_ready, 1)

            def decay_state(t):
                pool.wait_ge(out_ready, t + 1)
                if t:
                    pool.wait_ge(state_ready, t)
                nc.gpsimd.tensor_tensor(state[:, :, :], state[:, :, :], wide(cst[:, C_CD:C_CD + RETP], P), ALU.mult).then_inc(state_decayed, 1)

            jobs = {"turn_k": decay_q, "out2": decay_state}
            nc.gpsimd.memset(q_bd[:, :, :, :], 0.0).then_inc(zeroed, 1)
            pool.wait_ge(consts_ready, 4)
            for n in range(STEPS + 2):
                for m in at(n, WEIGH):
                    w = U[m].width
                    pool.wait_ge(scanned, m + 1)
                    pool.wait_ge(seeded, m + 1)
                    if m >= W3:
                        pool.wait_ge(w_turned, m - W3 + 1)
                    nc.gpsimd.tensor_tensor(w_t[:, m % W3, 0:w], beta[:, m % B, 0:w], stick[:, m % B, 1:w + 1], ALU.mult).then_inc(weighted, 1)
                for m in at(n, FOLD + 1):
                    u = U[m]
                    if u.last and u.h % 2:
                        pool.wait_ge(folded2, u.row + 1)
                        if u.t >= 2 and u.h == 1:
                            pool.wait_ge(o_stored[u.t % 2], 16 * (u.t // 2))
                        f = f2[:, u.row // 2 % 2, :]
                        nc.gpsimd.tensor_tensor(o_t[:, u.t % 2, u.h // 2, :], f[:, 0:P], f[:, P:2 * P], ALU.add).then_inc(folded, 1)
                for what, t in side.get(n - 1, ()):
                    if what in jobs:
                        jobs[what](t)



def emit(nc, cst, layer, proj, mixed, mem_k, mem_v, ret_norm_g, w_out, x_run):
    MT = MEM_TOKENS // P
    R, XR = 4, 3
    NR = RETP * P
    NVAR = NR + MEM_HEADS
    with Phase(nc, "emt") as ph:
        wo_raw = ph.sb("wo_raw", [P, ALLP, D_MODEL])
        wo_hi = ph.sb("wo_hi", [P, ALLP, D_MODEL], F32R)
        wo_lo = ph.sb("wo_lo", [P, ALLP, D_MODEL], F32R)
        k_raw = ph.sb("k_raw", [P, MEMP, MEM_TOKENS])
        kb_raw = ph.sb("kb_raw", [P, MEMP, 2, MEM_TOKENS])
        kb_hi = ph.sb("kb_hi", [P, MEMP, 2 * MEM_TOKENS], F32R)
        kb_lo = ph.sb("kb_lo", [P, MEMP, 2 * MEM_TOKENS], F32R)
        m_v = ph.sb("m_v", [P, MT, MEM_HEADS * HD])
        r_g = ph.sb("r_g", [P, RETP])
        m = ph.sb("m", [P, R, ALLP, P])
        g = ph.sb("g", [P, R, ALLP, P])
        x_t = ph.sb("x_t", [P, XR, D_MODEL])
        sq = ph.sb("sq", [P, RETP + MEMP, P])
        var, tmp = (ph.sb(n, [P, NVAR]) for n in ("var", "tmp"))
        root = ph.sb("root", [P, 2, NVAR])
        q_hi = ph.sb("q_hi", [P, 2, MEMP, P], F32R)
        q_lo = ph.sb("q_lo", [P, 2, MEMP, P], F32R)
        top, neg, total, inv = (ph.sb(n, [P, MEM_HEADS]) for n in ("top", "neg", "total", "inv"))
        prob = ph.sb("prob", [P, MEM_HEADS, MEM_TOKENS])
        prob_t = ph.sb("prob_t", [P, MEM_HEADS, MT, P])
        m_hi = ph.sb("m_hi", [P, 2, ALLP, P], F32R)
        m_lo = ph.sb("m_lo", [P, 2, ALLP, P], F32R)
        ps_var = ph.ps("ps_var", [P, 512])
        ps_att = ph.ps("ps_att", [P, 512])
        ps_s = ph.ps("ps_s", [P, MEM_HEADS, MEM_TOKENS])
        ps_y = [ph.ps(f"ps_y{i}", [P, 512]) for i in range(4)]

        names = ("consts_in kb_ready kbhi_ready kblo_ready whi_ready wlo_ready squared summed var_ready log_ready root0 dve rooted "
                 "normed qhi_ready qlo_ready scored top_ready exped prob_ready p_turned pt_ready attended gated_mix gated split_hi "
                 "split_lo y_ready added gain_ready").split()
        s = {n: ph.sem(n) for n in names}
        (consts_in, kb_ready, kbhi_ready, kblo_ready, whi_ready, wlo_ready, squared, summed, var_ready, log_ready, root0, dve, rooted,
         normed, qhi_ready, qlo_ready, scored, top_ready, exped, prob_ready, p_turned, pt_ready, attended, gated_mix, gated, split_hi,
         split_lo, y_ready, added, gain_ready) = (s[n] for n in names)
        w_loaded = [ph.sem(f"w_loaded{c}") for c in range(ALLP)]
        loaded = [ph.sem(f"loaded{i}") for i in range(R)]
        x_loaded = [ph.sem(f"x_loaded{i}") for i in range(XR)]
        stored = [ph.sem(f"stored{i}") for i in range(XR)]
        DMAS = 3
        block = ph.block()

        STEPS = range(-2, TILES)
        W_STEPS = (range(ALLP // 2), range(ALLP // 2, ALLP))

        def here(t):
            return 0 <= t < TILES

        @block.sync
        def _(sp):
            w_l = w_out[bass.ds(layer, 1)].rearrange("o (c p) n -> (o p) c n", p=P)
            mix_v = mixed.rearrange("(b p) n -> p b n", p=P)
            mem_q = proj[MEMQ * P:GATE0 * P, :].rearrange("(b p) n -> p b n", p=P)
            gates = proj[GATE0 * P:NBLK * P, :].rearrange("(b p) n -> p b n", p=P)

            def load(t):
                at, cols = t % R, slice(t * P, (t + 1) * P)
                if t >= R:
                    sp.wait_ge(split_lo, t - R + 1)
                sp.dma_start(m[:, at, 0:MIXP, :], mix_v[:, :, cols]).then_inc(loaded[at], 16)
                sp.dma_start(m[:, at, MIXP:ALLP, :], mem_q[:, :, cols]).then_inc(loaded[at], 16)
                sp.dma_start(g[:, at, :, :], gates[:, :, cols]).then_inc(loaded[at], 16)

            def load_x(t):
                if t >= XR:
                    sp.wait_ge(stored[t % XR], 16 * (t // XR))
                sp.dma_start(x_t[:, t % XR, :], x_run[t * P:(t + 1) * P, :]).then_inc(x_loaded[t % XR], 16)

            load(0)
            sp.dma_start(k_raw[:, :, :], mem_k[bass.ds(layer, 1)].rearrange("o p (a n) -> (o p) a n", a=MEMP)).then_inc(consts_in, 16)
            sp.dma_start(m_v[:, :, :], mem_v[bass.ds(layer, 1)].rearrange("o p (a n) -> (o p) a n", a=MT)).then_inc(consts_in, 16)
            sp.dma_start(r_g[:, :], ret_norm_g[bass.ds(layer, 1)].rearrange("o (c p) -> (o p) c", p=P),
                         allow_slow_non_contiguous=True).then_inc(consts_in, 16)
            for t in range(1, R):
                if t <= len(W_STEPS):
                    for c in W_STEPS[t - 1]:
                        sp.dma_start(wo_raw[:, c, :], w_l[:, c, :]).then_inc(w_loaded[c], 16)
                load(t)
            load_x(0)
            for t in range(TILES + 1):
                if here(t + R):
                    load(t + R)
                if here(t + 1):
                    load_x(t + 1)
                if t:
                    sp.wait_ge(added, 2 * t)
                    sp.dma_start(x_run[(t - 1) * P:t * P, :], x_t[:, (t - 1) % XR, :]).then_inc(stored[(t - 1) % XR], 16)
            for i in range(XR):
                sp.wait_ge(stored[i], 16 * len(range(i, TILES, XR)))

        @block.scalar
        def _(act):
            def square(t):
                act.wait_ge(loaded[t % R], 16 * DMAS * (t // R + 1))
                if t:
                    act.wait_ge(summed, t)
                nc.scalar.activation(sq[:, :, :], m[:, t % R, SBP:ALLP, :], ACT.Square).then_inc(squared, 1)

            def q_split(t):
                if t >= 2:
                    act.wait_ge(scored, t - 1)
                nc.scalar.copy(q_hi[:, t % 2, :, :], m[:, t % R, MIXP:ALLP, :]).then_inc(qhi_ready, 1)

            def roots(t):
                act.wait_ge(var_ready, t + 1)
                nc.scalar.activation(tmp[:, :], var[:, :], ACT.Ln).then_inc(log_ready, 1)
                act.wait_ge(log_ready, t + 1)
                nc.scalar.activation(root[:, t % 2, :], tmp[:, :], ACT.Exp, scale=-0.5).then_inc(root0, 1)

            def exps(t):
                act.wait_ge(top_ready, t + 1)
                if t:
                    act.wait_ge(p_turned, t)
                for h in range(MEM_HEADS):
                    nc.scalar.activation(prob[:, h, :], ps_s[:, h, :], ACT.Exp, bias=neg[:, h:h + 1],
                                         scale=root[:, t % 2, NR + h:NR + h + 1], accum_out=total[:, h:h + 1]).then_inc(exped, 1)

            def turned(t):
                act.wait_ge(p_turned, t + 1)
                if t:
                    act.wait_ge(attended, t)
                nc.scalar.copy(prob_t[:, :, :, :], ps_s[:, :, :].rearrange("p h (b n) -> p h b n", n=P)).then_inc(pt_ready, 1)

            def split(t):
                act.wait_ge(gated, t + 1)
                if t >= 2:
                    act.wait_ge(y_ready, 2 * (t - 1))
                nc.scalar.copy(m_hi[:, t % 2, :, :], m[:, t % R, :, :]).then_inc(split_hi, 1)

            nc.scalar.preload_act_table_set("natural_log_exp_and_others")
            square(0)
            q_split(0)
            act.wait_ge(kb_ready, 3)
            nc.scalar.copy(kb_hi[:, :, :], kb_raw[:, :, :, :].rearrange("p a b n -> p a (b n)")).then_inc(kbhi_ready, 1)
            for t in STEPS:
                if here(t + 1):
                    exps(t + 1)
                if here(t + 2):
                    roots(t + 2)
                if here(t + 3):
                    square(t + 3)
                    q_split(t + 3)
                if t < 0:
                    for c in W_STEPS[t + 2]:
                        act.wait_ge(w_loaded[c], 16)
                        nc.scalar.copy(wo_hi[:, c, :], wo_raw[:, c, :]).then_inc(whi_ready, 1)
                if here(t + 1):
                    turned(t + 1)
                    split(t + 1)

        @block.vector
        def _(v):
            n_dve = [0]

            def step(ins):
                n_dve[0] += 1
                ins.then_inc(dve, 1)
                v.wait_ge(dve, n_dve[0])

            def variance(t):
                v.wait_ge(summed, t + 1)
                if t:
                    v.wait_ge(rooted, t)
                nc.vector.tensor_scalar(var[:, :], ps_var[:, 0:NVAR], EPS, None, ALU.add).then_inc(var_ready, 1)

            def norm(t):
                v.wait_ge(root0, t + 1)
                v.wait_ge(var_ready, t + 1)
                r = root[:, t % 2, :]
                step(nc.vector.tensor_tensor(tmp[:, :], r, r, ALU.mult))
                step(nc.vector.scalar_tensor_tensor(tmp[:, :], tmp[:, :], -0.5, var[:, :], ALU.mult, ALU.mult))
                nc.vector.scalar_tensor_tensor(r, tmp[:, :], 1.5, r, ALU.add, ALU.mult).then_inc(rooted, 1)
                v.wait_ge(rooted, t + 1)
                nc.vector.tensor_tensor(m[:, t % R, SBP:MIXP, :], m[:, t % R, SBP:MIXP, :],
                                        r[:, 0:NR].rearrange("p (b n) -> p b n", n=P), ALU.mult).then_inc(normed, 1)

            def tops(t):
                v.wait_ge(scored, t + 1)
                step(nc.vector.tensor_reduce(top[:, :], ps_s[:, :, :], AX.X, ALU.max))
                nc.vector.scalar_tensor_tensor(neg[:, :], top[:, :], -1.0, root[:, t % 2, NR:NVAR], ALU.mult, ALU.mult).then_inc(top_ready, 1)

            def probs(t):
                v.wait_ge(exped, MEM_HEADS * (t + 1))
                step(nc.vector.reciprocal(inv[:, :], total[:, :]))
                for h in range(MEM_HEADS):
                    ins = nc.vector.tensor_scalar(prob[:, h, :], prob[:, h, :], inv[:, h:h + 1], None, ALU.mult)
                ins.then_inc(prob_ready, 1)

            def gate_mix(t):
                v.wait_ge(gain_ready, t + 1)
                v.wait_ge(normed, t + 1)
                nc.vector.tensor_tensor(m[:, t % R, 0:MIXP, :], m[:, t % R, 0:MIXP, :], g[:, t % R, 0:MIXP, :], ALU.mult).then_inc(gated_mix, 1)

            def gate_mem(t):
                v.wait_ge(attended, t + 1)
                v.wait_ge(qlo_ready, t + 1)
                v.wait_ge(squared, t + 1)
                nc.vector.tensor_tensor(m[:, t % R, MIXP:ALLP, :], ps_att[:, 0:MEMP * P].rearrange("p (b n) -> p b n", n=P),
                                        g[:, t % R, MIXP:ALLP, :], ALU.mult).then_inc(gated, 1)

            def add(t, half):
                v.wait_ge(y_ready, 2 * t + half + 1)
                if half == 0:
                    v.wait_ge(x_loaded[t % XR], 16 * (t // XR + 1))
                cols = slice(half * 512, (half + 1) * 512)
                nc.vector.tensor_tensor(x_t[:, t % XR, cols], ps_y[2 * (t % 2) + half][:, :], x_t[:, t % XR, cols], ALU.add).then_inc(added, 1)

            nc.vector.memset(kb_raw[:, :, :, :], 0.0).then_inc(kb_ready, 1)
            v.wait_ge(kb_ready, 1)
            v.wait_ge(consts_in, 48)
            for i in range(2):
                rows = slice(i * HD, (i + 1) * HD)
                nc.vector.tensor_copy(kb_raw[rows, :, i, :], k_raw[rows, :, :]).then_inc(kb_ready, 1)
            v.wait_ge(kbhi_ready, 1)
            nc.vector.tensor_tensor(kb_lo[:, :, :], kb_raw[:, :, :, :].rearrange("p a b n -> p a (b n)"), kb_hi[:, :, :],
                                    ALU.subtract).then_inc(kblo_ready, 1)
            for t in STEPS:
                if here(t + 1):
                    tops(t + 1)
                if here(t + 2):
                    variance(t + 2)
                if here(t - 1):
                    add(t - 1, 1)
                if here(t + 1):
                    gate_mix(t + 1)
                    probs(t + 1)
                if here(t + 2):
                    norm(t + 2)
                if t < 0:
                    for c in W_STEPS[t + 2]:
                        v.wait_ge(whi_ready, c + 1)
                        nc.vector.tensor_tensor(wo_lo[:, c, :], wo_raw[:, c, :], wo_hi[:, c, :], ALU.subtract).then_inc(wlo_ready, 1)
                if here(t):
                    add(t, 0)
                if here(t + 1):
                    gate_mem(t + 1)
            add(TILES - 1, 1)

        @block.gpsimd
        def _(pool):
            def gains(t):
                pool.wait_ge(loaded[t % R], 16 * DMAS * (t // R + 1))
                nc.gpsimd.tensor_tensor(g[:, t % R, SBP:MIXP, :], g[:, t % R, SBP:MIXP, :], wide(r_g[:, :], P), ALU.mult).then_inc(gain_ready, 1)

            def q_split(t):
                pool.wait_ge(qhi_ready, t + 1)
                if t >= 2:
                    pool.wait_ge(scored, t - 1)
                nc.gpsimd.tensor_tensor(q_lo[:, t % 2, :, :], m[:, t % R, MIXP:ALLP, :], q_hi[:, t % 2, :, :], ALU.subtract).then_inc(qlo_ready, 1)

            def split(t):
                pool.wait_ge(split_hi, t + 1)
                if t >= 2:
                    pool.wait_ge(y_ready, 2 * (t - 1))
                nc.gpsimd.tensor_tensor(m_lo[:, t % 2, :, :], m[:, t % R, :, :], m_hi[:, t % 2, :, :], ALU.subtract).then_inc(split_lo, 1)

            pool.wait_ge(consts_in, 48)
            gains(0)
            q_split(0)
            for t in STEPS:
                if here(t + 3):
                    gains(t + 3)
                    q_split(t + 3)
                if here(t + 1):
                    split(t + 1)

        @block.tensor
        def _(pe):
            def sums(t):
                pe.wait_ge(squared, t + 1)
                if t:
                    pe.wait_ge(var_ready, t)
                nc.tensor.matmul(ps_var[:, 0:NR], cst[:, C_AVG:C_AVG + P], sq[:, 0:RETP, :].rearrange("p b n -> p (b n)"), start=True, stop=True)
                for p in range(MEMP):
                    mm = nc.tensor.matmul(ps_var[:, NR + 2 * p:NR + 2 * p + 2], sq[:, RETP + p, :], cst[:, C_AVG:C_AVG + P:HD],
                                          start=True, stop=True)
                mm.then_inc(summed, 1)

            def scores(t):
                pe.wait_ge(qhi_ready, t + 1)
                pe.wait_ge(qlo_ready, t + 1)
                if t:
                    pe.wait_ge(pt_ready, t)
                for p in range(MEMP):
                    to = ps_s[:, 2 * p:2 * p + 2, :].rearrange("p h n -> p (h n)")
                    nc.tensor.matmul(to, q_hi[:, t % 2, p, :], kb_hi[:, p, :], start=True, stop=False)
                    nc.tensor.matmul(to, q_hi[:, t % 2, p, :], kb_lo[:, p, :], start=False, stop=False)
                    mm = nc.tensor.matmul(to, q_lo[:, t % 2, p, :], kb_hi[:, p, :], start=False, stop=True)
                mm.then_inc(scored, 1)

            def turn(t):
                pe.wait_ge(prob_ready, t + 1)
                for h in range(MEM_HEADS):
                    for b in range(MT):
                        mm = nc.tensor.transpose(ps_s[:, h, b * P:(b + 1) * P], prob[:, h, b * P:(b + 1) * P], cst[:, C_ID:C_ID + P])
                mm.then_inc(p_turned, 1)

            def attend(t):
                pe.wait_ge(pt_ready, t + 1)
                if t:
                    pe.wait_ge(gated, t)
                for h in range(MEM_HEADS):
                    rows = slice((h % 2) * HD, (h % 2 + 1) * HD)
                    for b in range(MT):
                        mm = nc.tensor.matmul(ps_att[rows, (h // 2) * P:(h // 2 + 1) * P], m_v[:, b, h * HD:(h + 1) * HD],
                                              prob_t[:, h, b, :], start=b == 0, stop=b == MT - 1)
                mm.then_inc(attended, 1)

            def project_part(t, part):
                half, quarter = part // 2, part % 2
                if part == 0:
                    pe.wait_ge(split_hi, t + 1)
                    pe.wait_ge(split_lo, t + 1)
                if quarter == 0 and t >= 2:
                    pe.wait_ge(added, 2 * (t - 2) + half + 1)
                cols = slice(half * 512, (half + 1) * 512)
                for c in range(quarter * ALLP // 2, (quarter + 1) * ALLP // 2):
                    if t == 0 and part < 2:
                        pe.wait_ge(wlo_ready, c + 1)
                    for i, (a, w) in enumerate(((m_hi, wo_hi), (m_hi, wo_lo), (m_lo, wo_hi))):
                        mm = nc.tensor.matmul(ps_y[2 * (t % 2) + half][:, :], a[:, t % 2, c, :], w[:, c, cols],
                                              start=c == 0 and i == 0, stop=c == ALLP - 1 and i == 2)
                if quarter == 1:
                    mm.then_inc(y_ready, 1)

            pe.wait_ge(consts_in, 48)
            pe.wait_ge(kbhi_ready, 1)
            pe.wait_ge(kblo_ready, 1)
            for t in STEPS:
                if here(t + 1):
                    scores(t + 1)
                if here(t + 2):
                    sums(t + 2)
                if here(t):
                    project_part(t, 0)
                    project_part(t, 1)
                if here(t + 1):
                    turn(t + 1)
                if here(t):
                    project_part(t, 2)
                if here(t + 1):
                    attend(t + 1)
                if here(t):
                    project_part(t, 3)



_INS = ["x", "mem", "positions", "norm_g", "w_in", "w_out", "mem_norm_g", "w_mem_kv", "mem_q_norm_g", "mem_k_norm_g", "ret_norm_g"]


def kernel(**inputs):
    import concourse.bacc as bacc
    from concourse.bass_utils import run_bass_kernel_spmd

    nc = bacc.Bacc("TRN2", target_bir_lowering=False, num_devices=1)
    arrays, args = {}, []
    for name in _INS:
        arrays[f"in_{name}"] = np.ascontiguousarray(inputs[name])
    arrays["in_consts"] = constants()
    for name, a in arrays.items():
        args.append(nc.dram_tensor(name, a.shape, mybir.dt.from_np(a.dtype), kind="ExternalInput").ap())
    out = nc.dram_tensor("out_x", (1, SEQ, D_MODEL), F32, kind="ExternalOutput").ap()
    build(nc, *args, out)
    r = run_bass_kernel_spmd(nc, [arrays], core_ids=[0])
    return r.results[0]["out_x"]
```
